# Optimizing a Trainium2 kernel written in Bass

```python
import math
import jax, jax.numpy as jnp
from jax import lax
import numpy as np

D_MODEL = 1024
BATCH = 1
SEQ = 256
DEPTH = 2

N_A_LAYERS = DEPTH // 2
N_B_LAYERS = DEPTH - N_A_LAYERS
DN_ALPHA = (2 * DEPTH) ** 0.25
DN_BETA = (8 * DEPTH) ** -0.25
LN_EPS = 1e-5

SSM_EXPAND = 2
SSM_D_INNER = SSM_EXPAND * D_MODEL
SSM_HEAD_DIM = 64
SSM_HEADS = SSM_D_INNER // SSM_HEAD_DIM
SSM_GROUPS = 4
SSM_STATE = 128
SSM_CONV = 4
SSM_CHUNK = 128
SSM_CONV_DIM = SSM_D_INNER + 2 * SSM_GROUPS * SSM_STATE
SSM_IN_DIM = SSM_D_INNER + SSM_CONV_DIM + SSM_HEADS

ATTN_HEAD_DIM = 64
ATTN_GROUPS = ((128, 1, 6), (512, 4, 5), (2048, 16, 5))
ATTN_HEADS = sum(g[2] for g in ATTN_GROUPS)
ATTN_WIDTH = ATTN_HEADS * ATTN_HEAD_DIM
ATTN_BLOCK = 128
N_BUCKETS = 32
MAX_DISTANCE = 2048

MOE_GROUPS = 4
MOE_EXPERTS_PER_GROUP = 8
MOE_TOP_K = 2
MOE_D_FF = 512

kernel_name = 'yoco_ssd_dilated_attn_hmoe'

def layer_norm(x, g, b):
    xf = x.astype(jnp.float32)
    mu = jnp.mean(xf, -1, keepdims=True)
    var = jnp.mean(jnp.square(xf - mu), -1, keepdims=True)
    return ((xf - mu) * lax.rsqrt(var + LN_EPS) * g.astype(jnp.float32) + b.astype(jnp.float32)).astype(x.dtype)

def causal_depthwise_conv(u, w, b):
    k, c = w.shape
    out = lax.conv_general_dilated(u, w[:, None, :], window_strides=(1,), padding=[(k - 1, 0)],
                                   dimension_numbers=('NWC', 'WIO', 'NWC'), feature_group_count=c)
    return out + b

def ssd_chunked(x, dt, a, bm, cm):
    b, s, h, p = x.shape
    g, n = bm.shape[2], bm.shape[3]
    r = h // g
    c = s // SSM_CHUNK
    xc = (x * dt[..., None].astype(x.dtype)).reshape(b, c, SSM_CHUNK, g, r, p)
    adt = (dt * a).reshape(b, c, SSM_CHUNK, g, r).transpose(0, 1, 3, 4, 2)
    acs = jnp.cumsum(adt, axis=-1)
    bc = bm.reshape(b, c, SSM_CHUNK, g, n)
    cc = cm.reshape(b, c, SSM_CHUNK, g, n)
    tri = np.tril(np.ones((SSM_CHUNK, SSM_CHUNK), dtype=bool))
    decay_in = jnp.exp(jnp.where(tri, acs[..., :, None] - acs[..., None, :], -jnp.inf))
    cb = jnp.einsum('bcign,bcjgn->bcgij', cc, bc)
    y_diag = jnp.einsum('bcgrij,bcjgrp->bcigrp', cb[:, :, :, None] * decay_in, xc)
    decay_states = jnp.exp(acs[..., -1:] - acs)
    states = jnp.einsum('bcjgn,bcgrj,bcjgrp->bcgrpn', bc, decay_states, xc)
    chunk_decay = jnp.exp(acs[..., -1])

    def step(carry, inp):
        st, dec = inp
        return carry * dec[..., None, None] + st, carry

    _, prev = lax.scan(step, jnp.zeros_like(states[:, 0]),
                       (jnp.swapaxes(states, 0, 1), jnp.swapaxes(chunk_decay, 0, 1)))
    prev = jnp.swapaxes(prev, 0, 1)
    y_off = jnp.einsum('bcign,bcgrpn,bcgri->bcigrp', cc, prev, jnp.exp(acs))
    return (y_diag + y_off).reshape(b, s, h, p)

def mamba2_mixer(h, in_w, conv_w, conv_b, dt_bias, a_log, d_skip, norm_w, out_w):
    bsz, s, _ = h.shape
    gn = SSM_GROUPS * SSM_STATE
    zxbcdt = h @ in_w
    z = zxbcdt[..., :SSM_D_INNER]
    xbc = zxbcdt[..., SSM_D_INNER:SSM_D_INNER + SSM_CONV_DIM]
    dt_raw = zxbcdt[..., SSM_D_INNER + SSM_CONV_DIM:]
    xbc = jax.nn.silu(causal_depthwise_conv(xbc, conv_w, conv_b))
    xs = xbc[..., :SSM_D_INNER].reshape(bsz, s, SSM_HEADS, SSM_HEAD_DIM)
    bm = xbc[..., SSM_D_INNER:SSM_D_INNER + gn].reshape(bsz, s, SSM_GROUPS, SSM_STATE)
    cm = xbc[..., SSM_D_INNER + gn:].reshape(bsz, s, SSM_GROUPS, SSM_STATE)
    dt = jax.nn.softplus(dt_raw.astype(jnp.float32) + dt_bias.astype(jnp.float32))
    a = -jnp.exp(a_log.astype(jnp.float32))
    y = ssd_chunked(xs, dt, a, bm, cm) + d_skip[:, None] * xs
    y = y.reshape(bsz, s, SSM_D_INNER) * jax.nn.silu(z)
    yg = y.astype(jnp.float32).reshape(bsz, s, SSM_GROUPS, -1)
    yg = yg * lax.rsqrt(jnp.mean(jnp.square(yg), -1, keepdims=True) + LN_EPS)
    y = (yg.reshape(bsz, s, SSM_D_INNER) * norm_w).astype(h.dtype)
    return y @ out_w

def t5_bucket(dist):
    max_exact = N_BUCKETS // 2
    n = np.maximum(dist, 1).astype(np.float64)
    large = max_exact + (np.log(n / max_exact) / np.log(MAX_DISTANCE / max_exact)
                         * (N_BUCKETS - max_exact)).astype(np.int32)
    large = np.minimum(large, N_BUCKETS - 1)
    return np.where(dist < max_exact, dist, large).astype(np.int32)

def dilated_group(q, k, v, bias_tab, window, dil):
    bsz, s, hg, dh = q.shape
    w_sub = window // dil
    l = s // dil
    nb = -(-l // ATTN_BLOCK)
    lp = nb * ATTN_BLOCK

    def split(t):
        return t.reshape(bsz, l, dil, hg, dh)

    qb = jnp.pad(split(q), ((0, 0), (0, lp - l), (0, 0), (0, 0), (0, 0))).reshape(bsz, nb, ATTN_BLOCK, dil, hg, dh)

    def kblocks(t):
        tp = jnp.pad(split(t), ((0, 0), (ATTN_BLOCK, lp - l), (0, 0), (0, 0), (0, 0)))
        tp = tp.reshape(bsz, nb + 1, ATTN_BLOCK, dil, hg, dh)
        return jnp.concatenate([tp[:, :-1], tp[:, 1:]], axis=2)

    kb, vb = kblocks(k), kblocks(v)
    sc = jnp.einsum('bnqrhe,bnkrhe->bnrhqk', qb, kb).astype(jnp.float32) * (ATTN_HEAD_DIM ** -0.5)
    delta = (np.arange(ATTN_BLOCK)[:, None] + ATTN_BLOCK) - np.arange(2 * ATTN_BLOCK)[None, :]
    band = (delta >= 0) & (delta <= w_sub)
    kpos = np.arange(nb)[:, None] * ATTN_BLOCK + np.arange(2 * ATTN_BLOCK)[None, :] - ATTN_BLOCK
    valid = band[None] & (kpos >= 0)[:, None, :]
    bucket = t5_bucket(np.clip(delta, 0, None) * dil)
    bias = jnp.transpose(bias_tab.astype(jnp.float32)[bucket], (2, 0, 1))
    sc = jnp.where(valid[None, :, None, None], sc + bias[None, None, None], -jnp.inf)
    m = jnp.max(sc, -1, keepdims=True)
    pr = jnp.exp(sc - m)
    den = jnp.sum(pr, -1)
    o = jnp.einsum('bnrhqk,bnkrhe->bnqrhe', pr.astype(v.dtype), vb)
    o = o / jnp.transpose(den, (0, 1, 4, 2, 3))[..., None]
    lse = jnp.transpose(m[..., 0] + jnp.log(den), (0, 1, 4, 2, 3))
    o = o.reshape(bsz, lp, dil, hg, dh)[:, :l].reshape(bsz, s, hg, dh)
    lse = lse.reshape(bsz, lp, dil, hg)[:, :l].reshape(bsz, s, hg)
    return o, lse

def dilated_attention(h, q_w, k_sh, v_sh, o_w, rel_bias):
    bsz, s, _ = h.shape
    q = (h @ q_w).reshape(bsz, s, ATTN_HEADS, ATTN_HEAD_DIM)
    outs, lses = [], []
    h0 = 0
    for window, dil, nh in ATTN_GROUPS:
        o, lse = dilated_group(q[:, :, h0:h0 + nh], k_sh[:, :, h0:h0 + nh], v_sh[:, :, h0:h0 + nh],
                               rel_bias[:, h0:h0 + nh], window, dil)
        outs.append(o)
        lses.append(jnp.mean(lse, -1))
        h0 += nh
    n_g = len(ATTN_GROUPS)
    wts = jax.nn.softmax(jnp.stack(lses, -1), -1) * n_g
    o = jnp.concatenate([outs[g] * wts[..., g, None, None] for g in range(n_g)], axis=2)
    return o.reshape(bsz, s, ATTN_WIDTH).astype(h.dtype) @ o_w

def hier_moe(h, group_w, group_b, expert_w, expert_b, gate_w, up_w, down_w):
    bsz, s, d = h.shape
    t = h.reshape(-1, d)
    g_logits = (t @ group_w).astype(jnp.float32) + group_b
    g_prob = jax.nn.softmax(g_logits, -1)
    g_idx = jnp.argmax(g_logits, -1)
    g_val = jnp.take_along_axis(g_prob, g_idx[:, None], -1)
    e_logits = jnp.einsum('nd,gde->nge', t, expert_w).astype(jnp.float32) + expert_b
    e_sel = jnp.take_along_axis(e_logits, g_idx[:, None, None], axis=1)[:, 0]
    top_v, top_i = lax.top_k(e_sel, MOE_TOP_K)
    top_p = jax.nn.softmax(top_v, -1) * g_val
    e_gate = jnp.sum(jax.nn.one_hot(top_i, MOE_EXPERTS_PER_GROUP, dtype=jnp.float32) * top_p[..., None], axis=1)
    gates = jax.nn.one_hot(g_idx, MOE_GROUPS, dtype=jnp.float32)[:, :, None] * e_gate[:, None, :]
    out = jnp.zeros((t.shape[0], d), jnp.float32)
    for g in range(MOE_GROUPS):
        hid = jax.nn.silu(jnp.einsum('nd,edf->nef', t, gate_w[g])) * jnp.einsum('nd,edf->nef', t, up_w[g])
        out = out + jnp.einsum('nef,efd->nd', hid * gates[:, g, :, None].astype(hid.dtype), down_w[g])
    return out.reshape(bsz, s, d).astype(h.dtype)

def setup_inputs(seed: int = 0) -> dict:
    key = jax.random.key(seed)
    ks = jax.random.split(key, 24)

    def nrm(k, shape, scale):
        return jax.random.normal(k, shape, jnp.float32) * scale

    na, nbl, L = N_A_LAYERS, N_B_LAYERS, DEPTH
    G, E, F = MOE_GROUPS, MOE_EXPERTS_PER_GROUP, MOE_D_FF
    x = nrm(ks[0], (BATCH, SEQ, D_MODEL), 1.0)
    ssm_in_w = nrm(ks[1], (na, D_MODEL, SSM_IN_DIM), D_MODEL ** -0.5)
    ssm_conv_w = nrm(ks[2], (na, SSM_CONV, SSM_CONV_DIM), SSM_CONV ** -0.5)
    ssm_conv_b = nrm(ks[3], (na, SSM_CONV_DIM), 0.02)
    dt0 = jnp.exp(jax.random.uniform(ks[4], (na, SSM_HEADS), jnp.float32, math.log(1e-3), math.log(1e-1)))
    ssm_dt_bias = dt0 + jnp.log(-jnp.expm1(-dt0))
    ssm_a_log = jnp.log(jax.random.uniform(ks[5], (na, SSM_HEADS), jnp.float32, 1.0, 16.0))
    ssm_d = 1.0 + nrm(ks[6], (na, SSM_HEADS), 0.1)
    ssm_norm_w = 1.0 + nrm(ks[7], (na, SSM_D_INNER), 0.05)
    ssm_out_w = nrm(ks[8], (na, SSM_D_INNER, D_MODEL), SSM_D_INNER ** -0.5 * DN_BETA)
    kv_w = jnp.concatenate([nrm(ks[9], (D_MODEL, ATTN_WIDTH), D_MODEL ** -0.5),
                            nrm(ks[10], (D_MODEL, ATTN_WIDTH), D_MODEL ** -0.5 * DN_BETA)], axis=1)
    attn_q_w = nrm(ks[11], (nbl, D_MODEL, ATTN_WIDTH), D_MODEL ** -0.5)
    attn_o_w = nrm(ks[12], (nbl, ATTN_WIDTH, D_MODEL), ATTN_WIDTH ** -0.5 * DN_BETA)
    rel_bias = nrm(ks[13], (N_BUCKETS, ATTN_HEADS), 0.5)
    moe_group_w = nrm(ks[14], (L, D_MODEL, G), D_MODEL ** -0.5)
    moe_group_b = nrm(ks[15], (L, G), 0.01)
    moe_expert_w = nrm(ks[16], (L, G, D_MODEL, E), D_MODEL ** -0.5)
    moe_expert_b = nrm(ks[17], (L, G, E), 0.01)
    moe_gate_w = nrm(ks[18], (L, G, E, D_MODEL, F), D_MODEL ** -0.5)
    moe_up_w = nrm(ks[19], (L, G, E, D_MODEL, F), D_MODEL ** -0.5 * DN_BETA)
    moe_down_w = nrm(ks[20], (L, G, E, F, D_MODEL), F ** -0.5 * DN_BETA)
    ln_g = 1.0 + nrm(ks[21], (L, 2, D_MODEL), 0.05)
    ln_b = nrm(ks[22], (L, 2, D_MODEL), 0.02)
    return {'x': x, 'ssm_in_w': ssm_in_w, 'ssm_conv_w': ssm_conv_w, 'ssm_conv_b': ssm_conv_b,
            'ssm_dt_bias': ssm_dt_bias, 'ssm_a_log': ssm_a_log, 'ssm_d': ssm_d, 'ssm_norm_w': ssm_norm_w,
            'ssm_out_w': ssm_out_w, 'kv_w': kv_w, 'attn_q_w': attn_q_w, 'attn_o_w': attn_o_w,
            'rel_bias': rel_bias, 'moe_group_w': moe_group_w, 'moe_group_b': moe_group_b,
            'moe_expert_w': moe_expert_w, 'moe_expert_b': moe_expert_b, 'moe_gate_w': moe_gate_w,
            'moe_up_w': moe_up_w, 'moe_down_w': moe_down_w, 'ln_g': ln_g, 'ln_b': ln_b}

def reference(x, ssm_in_w, ssm_conv_w, ssm_conv_b, ssm_dt_bias, ssm_a_log, ssm_d, ssm_norm_w,
              ssm_out_w, kv_w, attn_q_w, attn_o_w, rel_bias, moe_group_w, moe_group_b,
              moe_expert_w, moe_expert_b, moe_gate_w, moe_up_w, moe_down_w, ln_g, ln_b):
    bsz, s, _ = x.shape
    h = x
    k_sh = v_sh = None
    for i in range(DEPTH):
        if i < N_A_LAYERS:
            mix = mamba2_mixer(h, ssm_in_w[i], ssm_conv_w[i], ssm_conv_b[i], ssm_dt_bias[i],
                               ssm_a_log[i], ssm_d[i], ssm_norm_w[i], ssm_out_w[i])
        else:
            if i == N_A_LAYERS:
                kv = (h @ kv_w).reshape(bsz, s, 2, ATTN_HEADS, ATTN_HEAD_DIM)
                k_sh, v_sh = kv[:, :, 0], kv[:, :, 1]
            j = i - N_A_LAYERS
            mix = dilated_attention(h, attn_q_w[j], k_sh, v_sh, attn_o_w[j], rel_bias)
        h = layer_norm(DN_ALPHA * h + mix, ln_g[i, 0], ln_b[i, 0])
        ffn = hier_moe(h, moe_group_w[i], moe_group_b[i], moe_expert_w[i], moe_expert_b[i],
                       moe_gate_w[i], moe_up_w[i], moe_down_w[i])
        h = layer_norm(DN_ALPHA * h + ffn, ln_g[i, 1], ln_b[i, 1])
    return h


_drawn_inputs = setup_inputs


def setup_inputs(seed=0):
    import zlib

    import numpy as np

    out = dict(_drawn_inputs(seed))
    spreads = {}
    factors = {'ssm_conv_b': 5.473, 'ssm_norm_w': 3.015, 'moe_group_b': 147.679, 'moe_expert_b': 37.006}
    for name, (base, spread) in spreads.items():
        noise = np.random.default_rng([zlib.crc32(name.encode()), seed]).standard_normal(out[name].shape)
        drawn = base * np.exp(spread * noise) if base else spread * noise
        out[name] = __import__('jax').numpy.asarray(drawn.astype(out[name].dtype))
    for name, factor in factors.items():
        out[name] = (out[name] * factor).astype(out[name].dtype)
    return out
```

```python
import numpy as np
import concourse.bass as bass
from concourse import mybir
from contextlib import ExitStack

F32 = mybir.dt.float32
F32R = mybir.dt.float32r
ALU = mybir.AluOpType
ACT = mybir.ActivationFunctionType
AX = mybir.AxisListType

P = 128
D = 1024
S = 256
TB = S // P
KD = D // P
DI = 2048
NH = 32
HD = 64
G = 4
HG = NH // G
AH = 16
AGROUPS = ((0, 6), (6, 5), (11, 5))
E = 32
CAP = 64
NBLK = S // CAP
CAND = E * NBLK
NITEM = 44
assert CAND == P and NITEM >= E + (2 * S - E) // CAP + 5
RING = 6
SLOT = 4096
NSPLIT = 3
ALPHA = 4.0 ** 0.25
EPS = 1e-5
SCALE = HD ** -0.5

J_IN = 0
J_Z = J_IN + 6
J_OUT = J_Z + 8
J_MOE0 = J_OUT + 8
J_ATT = J_MOE0
J_MOE1 = J_ATT + 8

C_CW, C_CB, C_NW = 0, 96, 120
C_ID, C_TRI, C_STRI, C_ONE, C_IOTA = 136, 264, 392, 520, 648
C_RW = C_IOTA + 64
C_DTW = C_RW + 2 * KD * 36
C_REV = C_DTW + KD * NH
C_LNG = C_REV + P
C_LNB = C_LNG + 4 * KD
C_EXP = C_LNB + 4 * KD
C_THR = C_EXP + 1
C_END = C_THR + 1
R_DTB, R_AL, R_DS, R_RB = 0, 32, 64, 96
R_END = R_RB + 72


def program(nc, x, xT, consts, rows, in_w, out_w, kv_w, q_w, o_w, bias_pack, gate_w, up_w, down_w,
            ln_g, ln_b, out):
    ctx = ExitStack()
    with ctx:
        def sem(name):
            return ctx.enter_context(nc.semaphore(name))

        arena_words = 28400
        with nc.sbuf_tensor("split_ring", [P, RING, SLOT], F32R) as split_ring:
            pass
        ring = ctx.enter_context(nc.sbuf_tensor("ring", [P, RING, SLOT], F32))
        with nc.sbuf_tensor("split_arena", [P, arena_words], F32R) as split_arena:
            pass
        arena = ctx.enter_context(nc.sbuf_tensor("arena", [P, arena_words], F32))
        toeplitz_rows = nc.dram_tensor("toeplitz_rows", (AH, 384), F32).ap()
        bank = [ctx.enter_context(nc.psum_tensor(f"bank{i}", [P, 512], F32)) for i in range(8)]
        top = [0]

        def take(n):
            v = arena[:, top[0]:top[0] + n]
            top[0] += n
            assert top[0] <= arena_words
            return v

        cst = take(C_END)
        row = take(R_END)
        h_at = top[0]
        h = take(TB * D).rearrange("p (t d) -> p t d", t=TB)
        hT = take(KD * S).rearrange("p (k s) -> p k s", k=KD)
        lnw_at = top[0]
        lnw = take(2 * D).rearrange("p (a d) -> p a d", a=2)
        ident = cst[:, C_ID:C_ID + P]
        tri = cst[:, C_TRI:C_TRI + P]
        stri = cst[:, C_STRI:C_STRI + P]
        ones = cst[:, C_ONE:C_ONE + P]
        iota = cst[:, C_IOTA:C_IOTA + CAP]
        minus_half = take(TB)
        work = top[0]

        xtok_f = take(TB * DI)
        xtok = xtok_f.rearrange("p (g t c) -> p g t c", g=G, t=TB)
        y_at = top[0]
        y = take(TB * DI).rearrange("p (g t c) -> p g t c", g=G, t=TB)
        zs = take(2 * TB * 512).rearrange("p (b t c) -> p b t c", b=2, t=TB)
        bcT = take(8 * S).rearrange("p (k s) -> p k s", k=8)
        cbm = take(TB * G * P).rearrange("p (c g i) -> p c g i", c=TB, g=G)
        dec = take(2 * HG * P).rearrange("p (c r i) -> p c r i", c=2, r=HG)
        btok = take(G * P).rearrange("p (g n) -> p g n", g=G)
        xw = take(512)
        xd = take(TB * 512).rearrange("p (t c) -> p t c", t=TB)
        stT = take(512)
        conv_acc = take(2 * S).rearrange("p (b s) -> p b s", b=2)
        xcm = take(2 * S).rearrange("p (b s) -> p b s", b=2)
        dts = take(10 * TB * NH).rearrange("p (a t h) -> p a t h", a=10, t=TB)
        sq = take(512)
        stats = take(64)

        yT_high = split_arena[:, work:work + TB * DI].rearrange("p (k s) -> p k s", s=S)
        yT_low = split_arena[:, y_at:y_at + TB * DI].rearrange("p (k s) -> p k s", s=S)
        xT_high = split_arena[:, h_at:h_at + KD * S].rearrange("p (k s) -> p k s", k=KD)
        xT_low = split_arena[:, lnw_at:lnw_at + KD * S].rearrange("p (k s) -> p k s", k=KD)
        w_split = split_arena[:, y_at:y_at + NSPLIT * 2 * D].rearrange("p (b a k c) -> p b a k c",
                                                                       b=NSPLIT, a=2, k=KD)

        top[0] = work
        sel = take(TB * P).rearrange("p (t c) -> p t c", t=TB)
        selg = take(TB * P).rearrange("p (t c) -> p t c", t=TB)
        exT = take(KD * P).rearrange("p (k c) -> p k c", k=KD)
        silu_g = take(512)
        hid = take(512)
        hidT = take(512).rearrange("p (k c) -> p k c", k=4)
        selgT = take(S)
        yex = take(D)
        yacc = take(TB * D).rearrange("p (t d) -> p t d", t=TB)
        rank_item = take(TB * NITEM).rearrange("p (t i) -> p t i", t=TB)
        gate_item = take(TB * NITEM).rearrange("p (t i) -> p t i", t=TB)
        tables = take(2 * TB * CAND).rearrange("p (a t c) -> p a t c", a=2, t=TB)
        tablesT = take(2 * TB * P)
        is_item = take(NITEM)
        rt = take(1400)
        lnst = take(64)
        after_moe = top[0]
        moe_top = top[0]

        top[0] = arena_words - 4096
        bias = take(AH * S).rearrange("p (h c) -> p h c", h=AH)
        top[0] = work
        qT = take(KD * S).rearrange("p (k s) -> p k s", k=KD)
        kT = take(KD * S).rearrange("p (k s) -> p k s", k=KD)
        v = take(TB * D).rearrange("p (t d) -> p t d", t=TB)
        osb = take(TB * D).rearrange("p (t d) -> p t d", t=TB)
        oT = take(KD * S).rearrange("p (k s) -> p k s", k=KD)
        scb = take(2 * 384).rearrange("p (b c) -> p b c", b=2)
        pT = take(2 * 384).rearrange("p (b c) -> p b c", b=2)
        am = take(12 * 32).rearrange("p (a q h) -> p a q h", a=12, q=2)
        lnst2 = take(64)
        assert top[0] <= arena_words - 4096 and moe_top <= arena_words - 4096
        small = ctx.enter_context(nc.sbuf_tensor("small", [P, 2, NITEM + 1], mybir.dt.int32))
        idx = ctx.enter_context(nc.sbuf_tensor("idx", [P, 32], mybir.dt.uint32))
        dec_flat = dec.rearrange("p c r i -> p (c r i)")
        bp = dec_flat[0:32, 0:384 * 2 + AH]
        trow = dec_flat[0:AH, 1024:1024 + 384]

        w_full = [sem(f"w_full{i}") for i in range(RING)]
        piece_low = sem("piece_low")
        w_used = sem("w_used")
        x_in, c_in, r_in, h_in, b_in = (sem(n) for n in ("x_in", "c_in", "r_in", "h_in", "b_in"))
        ln_in = sem("ln_in")
        ln_used = sem("ln_used")
        dve_c, act_c, pool_c = sem("dve_c"), sem("act_c"), sem("pool_c")
        dt_mm, dt_a, dt_b, dt_c, dt_dve, acs_mm, dt_ready = (sem(n) for n in (
            "dt_mm", "dt_a", "dt_b", "dt_c", "dt_dve", "acs_mm", "dt_ready"))
        x_high, x_low = sem("x_high"), sem("x_low")
        w_high, w_low_p, w_low_v = sem("w_high"), sem("w_low_p"), sem("w_low_v")
        ch_mm, ch_seed, ch_conv, ch_silu = sem("ch_mm"), sem("ch_seed"), sem("ch_conv"), sem("ch_silu")
        cb_mm, cb_ready, btok_mm, btok_ready = sem("cb_mm"), sem("cb_ready"), sem("btok_mm"), sem("btok_ready")
        xt_mm, xt_ready = sem("xt_mm"), sem("xt_ready")
        dec_mm, dec_sub, dec_exp, dec_ready = sem("dec_mm"), sem("dec_sub"), sem("dec_exp"), sem("dec_ready")
        z_mm, z_ready, xw_ready, xd_ready = sem("z_mm"), sem("z_ready"), sem("xw_ready"), sem("xd_ready")
        st_mm, st_ready, yd_mm, yo_mm, y_gated, y_sq, y_ready = (sem(n) for n in (
            "st_mm", "st_ready", "yd_mm", "yo_mm", "y_gated", "y_sq", "y_ready"))
        yT_mm, yT_ready, yT_rest = sem("yT_mm"), sem("yT_ready"), sem("yT_rest")
        tb_mm, tb_row, tb_out, tb_in = sem("tb_mm"), sem("tb_row"), sem("tb_out"), sem("tb_in")
        var_ready, rstd_ready = sem("var_ready"), sem("rstd_ready")
        mix_mm = sem("mix_mm")
        h_ready = sem("h_ready")
        h_final = [sem(f"h_final{t}") for t in range(TB)]
        xn_ready = sem("xn_ready")
        hT_mm = sem("hT_mm")
        hT_a, hT_v = sem("hT_a"), sem("hT_v")
        out_done = sem("out_done")
        att = {n: sem("att_" + n) for n in (
            "rev", "bias", "proj", "ev_a", "ev_v", "score", "logit", "negmax", "prob", "pt", "ptc", "pv", "oc",
            "ln", "lse", "wexp", "o", "oT", "oTa", "oTv")}
        moe = [{n: sem(f"moe{L}_" + n) for n in (
            "logit", "gsub", "gexp", "dsub", "dexp", "mask", "rank", "active", "place", "table", "turned",
            "turnedc", "item", "listed", "route", "sel", "gathered",
            "exT_a", "exT_v", "gate", "silu", "up", "hid", "tr", "hidT", "selgT", "down", "yex_a",
            "yex_v", "comb", "added", "end")} for L in range(2)]

        block = ctx.enter_context(nc.Block())

        def in_order(eng, s):
            n = [0]

            def link(ins):
                n[0] += 1
                ins.then_inc(s, 1)
                eng.wait_ge(s, n[0])
            return link

        def cols(w, c):
            return w[:, c:c + 512].rearrange("(k p) n -> p k n", p=P)

        def krows(w, r):
            return w[r:r + 512, :].rearrange("(k p) n -> p k n", p=P)

        def wide(j):
            return ring[:, j % RING, :].rearrange("p (k n) -> p k n", k=KD)

        def tall(j):
            return ring[:, j % RING, :].rearrange("p (k n) -> p k n", k=4)

        in_cols = [4096, 4608, 2048, 2560, 3072, 3584, 0, 512, 1024, 1536]
        pre = [(J_IN + i, wide, cols(in_w, c)) for i, c in enumerate(in_cols[:6])]
        pre += [(J_Z + 2 * i, wide, cols(in_w, c)) for i, c in enumerate(in_cols[6:])]
        pre += [(J_OUT + 2 * i, tall, krows(out_w, 512 * i)) for i in range(4)]
        mid = [(J_ATT, wide, cols(kv_w, 0)), (J_ATT + 1, wide, cols(q_w, 0)),
               (J_ATT + 2, wide, cols(kv_w, 1024)), (J_ATT + 3, wide, cols(kv_w, 1536)),
               (J_ATT + 4, wide, cols(kv_w, 512)), (J_ATT + 5, wide, cols(q_w, 512))]
        mid += [(J_ATT + 6 + i, tall, krows(o_w, 512 * i)) for i in (0, 1)]

        def unit_buffer(u):
            kind, n = UNITS[u][:2]
            if kind == "V":
                return v[:, n % 2, (n // 2) * 512:(n // 2 + 1) * 512]
            return (kT if kind == "K" else qT)[:, n, :]

        def further_pairs(eng, L):
            return eng.value_load(small[0:1, L, NITEM:NITEM + 1], min_val=3, max_val=NITEM // 2 - 3)

        def split_low(eng, unit, i, done):
            eng.wait_ge(w_high, i)
            unit.tensor_tensor(w_split[:, i % NSPLIT, 1], wide(J_IN + i // 4)[:, :, (i % 4) * P:(i % 4 + 1) * P],
                               w_split[:, i % NSPLIT, 0], ALU.subtract).then_inc(done, 1)

        @block.sync
        def _(sp):
            sp.dma_start(hT[:, :, :], xT).then_inc(x_in, 16)

            def load(j, shape, src, pairs=None):
                if j >= RING:
                    n = j - RING + 1
                    sp.wait_ge(w_used, n if pairs is None else pairs * 6 + n)
                sp.dma_start(shape(j), src).then_inc(w_full[j % RING], 16)

            def load_pair(L, base, q, experts):
                for i, (w, shape) in enumerate(((gate_w, wide), (gate_w, wide), (up_w, wide), (up_w, wide),
                                                (down_w, tall), (down_w, tall))):
                    j = base + i
                    sp.wait_ge(w_used, q * 6 + (j - RING + 1))
                    src = w[L, bass.ds(experts[i % 2], 1)].rearrange("e (k p) n -> p (e k) n", p=P)
                    sp.dma_start(shape(j), src).then_inc(w_full[j % RING], 16)

            def load_moe(L, base, before):
                load_pair(L, base, before, (0, 1))
                sp.wait_ge(moe[L]["route"], 1)
                further = further_pairs(sp, L)
                with sp.Fori(0, further) as p:
                    e = [sp.value_load(small[0:1, L, bass.ds(p * 2 + 2 + i, 1)], min_val=0, max_val=E - 1)
                         for i in range(2)]
                    load_pair(L, base, p + (before + 1), e)
                return further + (before + 1)

            for j, shape, src in pre:
                load(j, shape, src)
                if j == 0:
                    sp.dma_start(cst[:, :], consts).then_inc(c_in, 16)
            pairs0 = load_moe(0, J_MOE0, 0)
            for j, shape, src in mid:
                load(j, shape, src, pairs0)
            load_moe(1, J_MOE1, pairs0)
            for t in range(TB):
                sp.wait_ge(h_final[t], 1)
                sp.dma_start(out[0, t * P:(t + 1) * P, :], h[:, t, :]).then_inc(out_done, 16)
            sp.wait_ge(out_done, 16 * TB)

        def filled(eng, j, pairs=None):
            n = 16 * (j // RING + 1)
            eng.wait_ge(w_full[j % RING], n if pairs is None else pairs * 16 + n)

        CH = SLOT // 4

        def high_chunk(act, j, c, pairs=None):
            if c == 0:
                filled(act, j, pairs)
                n = j + 1 - RING + 1
                act.wait_ge(w_used, n if pairs is None else pairs * 6 + n)
            nc.scalar.activation(split_ring[:, (j + 1) % RING, c * CH:(c + 1) * CH],
                                 ring[:, j % RING, c * CH:(c + 1) * CH], ACT.Copy).then_inc(w_full[(j + 1) % RING], 4)

        def low_chunk(pool, j, c, pairs=None):
            n = 16 * ((j + 1) // RING) + 4 * (c + 1)
            pool.wait_ge(w_full[(j + 1) % RING], n if pairs is None else pairs * 16 + n)
            here = slice(c * CH, (c + 1) * CH)
            nc.gpsimd.tensor_tensor(split_ring[:, j % RING, here], ring[:, j % RING, here],
                                    split_ring[:, (j + 1) % RING, here], ALU.subtract).then_inc(piece_low, 1)

        def high_low(j, k_tiles):
            return [split_ring[:, jj % RING, :].rearrange("p (k n) -> p k n", k=k_tiles) for jj in (j + 1, j)]

        def token_transposes(pe, src, first_bank, done):
            for k in range(KD):
                for t in range(TB):
                    b = bank[first_bank + k // 2]
                    c = (k % 2) * S + t * P
                    last = nc.tensor.transpose(b[:, c:c + P], src[:, t, k * P:(k + 1) * P], ident)
                if k % 2:
                    last.then_inc(done, 1)

        @block.tensor
        def _(pe):
            mm = nc.tensor.matmul
            pe.wait_ge(x_in, 16)

            def channel_tile(i):
                j = J_IN + i // 4
                if i % 4 == 0:
                    filled(pe, j)
                if i >= 2:
                    pe.wait_ge(ch_conv, i - 1)
                if i == 0:
                    for k in range(KD):
                        last = mm(bank[0][:, 0:S], wide(j)[:, k, 0:P], hT[:, k, :], start=k == 0, stop=k == KD - 1)
                else:
                    if i == 1:
                        pe.wait_ge(x_low, 1)
                    if i % 3 == 0:
                        pe.wait_ge(w_low_v, i // 3)
                    else:
                        pe.wait_ge(w_low_p, i - i // 3)
                    high, low = w_split[:, i % NSPLIT, 0], w_split[:, i % NSPLIT, 1]
                    for n, (w, a) in enumerate(((high, xT_high), (high, xT_low), (low, xT_high))):
                        for k in range(KD):
                            last = mm(bank[i % 2][:, 0:S], w[:, k, :], a[:, k, :], start=n == 0 and k == 0,
                                      stop=n == 2 and k == KD - 1)
                last.then_inc(ch_mm, 1)
                if i % 4 == 3:
                    pe.drain().then_inc(w_used, 1)

            def xs_transpose(i):
                pe.wait_ge(ch_silu, 8 + i + 1)
                if i >= 2:
                    pe.wait_ge(xt_ready, i - 1)
                for t in range(TB):
                    last = nc.tensor.transpose(bank[4 + i % 2][:, t * P:(t + 1) * P],
                                               xcm[:, i % 2, t * P:(t + 1) * P], ident)
                last.then_inc(xt_mm, 1)

            for i in range(8):
                channel_tile(i)
                if i == 1:
                    pe.wait_ge(c_in, 16)
                    for t in range(TB):
                        for k in range(KD):
                            last = mm(bank[6][:, t * NH:(t + 1) * NH], hT[:, k, t * P:(t + 1) * P],
                                      cst[:, C_DTW + k * NH:C_DTW + (k + 1) * NH], start=k == 0, stop=k == KD - 1)
                    last.then_inc(dt_mm, 1)
                    pe.wait_ge(b_in, 16)
                    mm(bank[7][0:AH, 0:384], bp[:, 768:768 + AH], bp[:, 0:384], start=True,
                       stop=True).then_inc(tb_mm, 1)
            pe.wait_ge(dt_ready, 1)
            pe.wait_ge(tb_row, 1)
            for t in range(TB):
                mm(bank[7][:, t * NH:(t + 1) * NH], tri, dts[:, 2, t, :], start=True, stop=True)
            mm(bank[7][:, 64:64 + NH], ones, dts[:, 2, 0, :], start=True, stop=True).then_inc(acs_mm, 1)
            channel_tile(8)
            pe.wait_ge(ch_silu, 8)
            for c in range(TB):
                for g in range(G):
                    last = mm(bank[4 + c][:, g * P:(g + 1) * P], bcT[:, g, c * P:(c + 1) * P],
                              bcT[:, G + g, c * P:(c + 1) * P], start=True, stop=True)
            last.then_inc(cb_mm, 1)
            for g in range(G):
                last = nc.tensor.transpose(bank[6][:, g * P:(g + 1) * P], bcT[:, g, 0:P], ident)
            last.then_inc(btok_mm, 1)
            channel_tile(9)
            for i in range(10, 24):
                if i == 11:
                    pe.wait_ge(cb_ready, 1)
                    xs_transpose(0)
                if i > 10:
                    xs_transpose(i - 10)
                channel_tile(i)

            def y_transposes(g, first_bank):
                pe.wait_ge(y_ready, g + 1)
                for i in range(4 * g, 4 * g + 4):
                    for t in range(TB):
                        c = (i % 2) * S + t * P
                        last = nc.tensor.transpose(bank[first_bank + (i % 4) // 2][:, c:c + P],
                                                   y[:, g, t, (i % 4) * P:(i % 4 + 1) * P], ident)
                last.then_inc(yT_mm, 1)

            def z_tile(g, t):
                j = J_Z + 2 * g
                if g:
                    pe.wait_ge(z_ready, g)
                    pe.wait_ge(y_gated, g)
                w_high_, w_low_ = high_low(j, KD)
                for k in range(KD):
                    if k % 2 == 0:
                        pe.wait_ge(piece_low, 4 * g + k // 2 + 1)
                    for n, (a, w) in enumerate(((xT_high, w_high_), (xT_low, w_high_), (xT_high, w_low_))):
                        mm(bank[2 + t][:, :], a[:, k, t * P:(t + 1) * P], w[:, k, :], start=k == 0 and n == 0,
                           stop=k == KD - 1 and n == 2)

            z_tile(0, 0)
            xs_transpose(14)
            xs_transpose(15)
            pe.wait_ge(xt_ready, 16)
            pe.wait_ge(btok_ready, 1)
            for g in range(G):
                if g:
                    pe.wait_ge(st_ready, g)
                if g >= 2:
                    pe.wait_ge(yT_rest, 4 * (g - 1))
                for c in range(TB):
                    for r in range(HG):
                        b = bank[4 + 2 * c + r // 4]
                        a = dts[:, 2, c, g * HG + r:g * HG + r + 1]
                        last = mm(b[:, (r % 4) * P:(r % 4 + 1) * P], a.to_broadcast([P, P]), tri,
                                  start=True, stop=True)
                last.then_inc(dec_mm, 1)
                z_tile(g, 1)
                if g:
                    z_tile(g, 0)
                pe.drain().then_inc(z_mm, 1)
                pe.drain().then_inc(w_used, 2)
                pe.wait_ge(xw_ready, g + 1)
                pe.wait_ge(dec_sub, g + 1)
                mm(bank[4][:, :], btok[:, g, :], xw[:, :], start=True, stop=True).then_inc(st_mm, 1)
                if g:
                    y_transposes(g - 1, 6)
                pe.wait_ge(dec_ready, g + 1)
                for c in range(TB):
                    for r in range(HG):
                        last = mm(bank[c][:, r * HD:(r + 1) * HD], dec[:, c, r, :],
                                  xtok[:, g, c, r * HD:(r + 1) * HD], start=True, stop=True)
                last.then_inc(yd_mm, 1)
                pe.wait_ge(st_ready, g + 1)
                pe.wait_ge(z_ready, g + 1)
                mm(bank[3][:, :], bcT[:, G + g, P:2 * P], stT[:, :], start=True, stop=True).then_inc(yo_mm, 1)
            pe.wait_ge(yT_rest, 12)
            for i in range(DI // P):
                j = J_OUT + 2 * (i // 4)
                pe.wait_ge(piece_low, 16 + i + 1)
                if i == 12:
                    y_transposes(3, 0)
                    pe.wait_ge(yT_rest, 16)
                w_high_, w_low_ = high_low(j, 4)
                for t in range(TB):
                    for n, (a, w) in enumerate(((yT_high, w_high_), (yT_high, w_low_), (yT_low, w_high_))):
                        for c in range(2):
                            mm(bank[4 + 2 * t + c][:, :], a[:, i, t * P:(t + 1) * P],
                               w[:, i % 4, c * 512:(c + 1) * 512], start=i == 0 and n == 0,
                               stop=i == 15 and n == 2, skip_group_check=True)
                if i % 4 == 3:
                    pe.drain().then_inc(w_used, 2)
            pe.drain().then_inc(mix_mm, 1)

            def normed(n):
                for t in range(TB):
                    pe.wait_ge(xn_ready, (n - 1) * TB + t + 1)
                    for k in range(KD):
                        c = (k % 2) * S + t * P
                        last = nc.tensor.transpose(bank[4 + k // 2][:, c:c + P], h[:, t, k * P:(k + 1) * P], ident)
                        if t == TB - 1 and k % 2:
                            last.then_inc(hT_mm, 1)
                pe.wait_ge(hT_a, 2 * n)
                pe.wait_ge(hT_v, 2 * n)

            def gather(m, wait):
                pe.wait_ge(m["sel"], wait)
                for k in range(KD):
                    for t in range(TB):
                        last = mm(bank[k // 4][:, (k % 4) * P:(k % 4 + 1) * P], h[:, t, k * P:(k + 1) * P],
                                  sel[:, t, :], start=t == 0, stop=t == TB - 1)
                last.then_inc(m["gathered"], 1)

            def expert_pair(L, base, q, before, following):
                m = moe[L]
                pe.wait_ge(m["exT_a"], q + 1)
                pe.wait_ge(m["exT_v"], q + 1)

                def piece(j):
                    filled(pe, j, q if before is None else q + before)

                for first, out_bank, name in ((0, 2, "gate"), (2, 3, "up")):
                    for k in range(KD):
                        for e in range(2):
                            if k == 0:
                                piece(base + first + e)
                            last = mm(bank[out_bank][64 * e:64 * e + 64, :], exT[:, k, 64 * e:64 * e + 64],
                                      wide(base + first + e)[:, k, :], start=k == 0, stop=k == KD - 1)
                            if k == KD - 1 and e == 0:
                                last.then_inc(w_used, 1)
                    last.then_inc(m[name], 1)
                    pe.drain().then_inc(w_used, 1)
                if following:
                    gather(m, q + 2)
                pe.wait_ge(m["hid"], q + 2)
                pe.wait_ge(m["added"], q * 4 + 1)
                for k in range(4):
                    nc.tensor.transpose(bank[4][:, k * P:(k + 1) * P], hid[:, k * P:(k + 1) * P], ident)
                for t in range(TB):
                    last = nc.tensor.transpose(bank[7][:, t * P:(t + 1) * P], selg[:, t, :], ident)
                last.then_inc(m["tr"], 1)
                pe.wait_ge(m["hidT"], q + 1)
                for k in range(4):
                    for c in range(2):
                        for e in range(2):
                            if k == 0 and c == 0:
                                piece(base + 4 + e)
                            last = mm(bank[5 + c][64 * e:64 * e + 64, :], hidT[:, k, 64 * e:64 * e + 64],
                                      tall(base + 4 + e)[:, k, c * 512:(c + 1) * 512], start=k == 0, stop=k == 3,
                                      skip_group_check=True)
                            if k == 3 and c == 1 and e == 0:
                                last.then_inc(w_used, 1)
                last.then_inc(m["down"], 1)
                pe.drain().then_inc(w_used, 1)
                pe.wait_ge(m["selgT"], q + 1)
                for i, (t, c) in enumerate(((0, 0), (0, 1), (1, 0), (1, 1))):
                    if i == 0:
                        pe.wait_ge(m["yex_a"], q + 1)
                    if i == 1:
                        pe.wait_ge(m["yex_v"], q + 1)
                    if i >= 2:
                        pe.wait_ge(m["added"], q * 4 + i)
                    mm(bank[7 if i % 2 == 0 else 4][:, :], selgT[:, t * P:(t + 1) * P],
                       yex[:, c * 512:(c + 1) * 512], start=True, stop=True).then_inc(m["comb"], 1)

            def experts(L, base, before):
                m = moe[L]
                for t in range(TB):
                    for k in range(KD):
                        c = C_RW + (L * KD + k) * 36
                        last = mm(bank[0][:, t * 36:(t + 1) * 36], hT[:, k, t * P:(t + 1) * P], cst[:, c:c + 36],
                                  start=k == 0, stop=k == KD - 1)
                last.then_inc(m["logit"], 1)
                pe.wait_ge(m["mask"], 1)
                mask = rt[:, 0:TB * E].rearrange("p (t e) -> p t e", t=TB)
                b = bank[4]
                mm(b[:, 0:E], stri, mask[:, 0, :], start=True, stop=True)
                mm(b[:, E:2 * E], stri, mask[:, 1, :], start=True, stop=False)
                mm(b[:, E:2 * E], ones, mask[:, 0, :], start=False, stop=True)
                for i in range(NBLK):
                    for t in range(TB):
                        last = mm(b[i * E:(i + 1) * E, 2 * E:2 * E + 1], mask[:, t, :], ones[:, 0:1],
                                  start=t == 0, stop=t == TB - 1)
                last.then_inc(m["rank"], 1)
                pe.wait_ge(h_ready, L * 2 + 1)
                gather(m, 1)
                pe.wait_ge(m["active"], 1)
                active = rt[:, 380:381]
                mm(bank[5][:, 0:1], stri, active, start=True, stop=True).then_inc(m["place"], 1)
                pe.wait_ge(m["table"], 1)
                for a in range(2):
                    for t in range(TB):
                        c = (a * TB + t) * P
                        last = nc.tensor.transpose(bank[6][:, c:c + P], tables[:, a, t, :], ident)
                last.then_inc(m["turned"], 1)
                pe.wait_ge(m["item"], 1)
                mm(bank[5][0:1, 64:64 + NITEM], cst[:, C_EXP:C_EXP + 1], is_item, start=True, stop=True)
                mm(bank[5][0:1, 128:128 + NITEM], ones[:, 0:1], is_item, start=True, stop=True)
                pe.wait_ge(m["turnedc"], 1)
                for i in range(2 * TB):
                    last = mm(bank[7][:, i * NITEM:(i + 1) * NITEM], tablesT[:, i * P:(i + 1) * P], is_item,
                              start=True, stop=True)
                last.then_inc(m["listed"], 1)
                pe.wait_ge(m["route"], 1)
                further = further_pairs(pe, L)
                with pe.Fori(0, further) as q:
                    expert_pair(L, base, q, before, True)
                expert_pair(L, base, further, before, False)
                return further + 1

            normed(1)
            pairs0 = experts(0, J_MOE0, None)
            pe.wait_ge(tb_in, 16)
            for i in range(8):
                if i >= 2:
                    pe.wait_ge(att["bias"], i - 1)
                mm(bank[i % 2][:, :], cst[:, C_REV:C_REV + P], bias[:, 2 * i:2 * i + 2, :], start=True,
                   stop=True).then_inc(att["rev"], 1)
            normed(2)

            def project(u):
                kind, n, j, first, last_use = UNITS[u]
                if u == 0:
                    pe.wait_ge(att["bias"], 8)
                if u >= 2:
                    pe.wait_ge(att["ev_a"] if u % 2 == 0 else att["ev_v"], (u - 2) // 2 + 1)
                if first:
                    filled(pe, j, pairs0)
                for k in range(KD):
                    if kind == "V":
                        last = mm(bank[u % 2][:, :], hT[:, k, (n % 2) * P:(n % 2 + 1) * P], wide(j)[:, k, :],
                                  start=k == 0, stop=k == KD - 1)
                    else:
                        last = mm(bank[u % 2][:, 0:S], wide(j)[:, k, (n % 4) * P:(n % 4 + 1) * P], hT[:, k, :],
                                  start=k == 0, stop=k == KD - 1)
                last.then_inc(att["proj"], 1)
                if last_use:
                    pe.drain().then_inc(w_used, 1)

            def projected(u):
                pe.wait_ge(att["ev_a"], u // 2 + 1)
                pe.wait_ge(att["ev_v"], (u + 1) // 2)

            def scores(n):
                projected(UNIT_OF_HEADS[n // 2])
                if n >= 2:
                    pe.wait_ge(att["prob"], n - 1)
                b, r, k = bank[4 + n % 2], HD * (n % 2), n // 2
                mm(b[:, 0:P], qT[r:r + HD, k, 0:P], kT[r:r + HD, k, 0:P], start=True, stop=True)
                mm(b[:, P:P + S], qT[r:r + HD, k, P:S], kT[r:r + HD, k, :], start=True,
                   stop=True).then_inc(att["score"], 1)

            def turn(n):
                pe.wait_ge(att["prob"], n + 1)
                if n >= 2:
                    pe.wait_ge(att["ptc"], n - 1)
                for i in range(3):
                    last = nc.tensor.transpose(bank[6 + n % 2][:, i * P:(i + 1) * P],
                                               scb[:, n % 2, i * P:(i + 1) * P], ident)
                last.then_inc(att["pt"], 1)

            def values(n):
                projected(UNIT_OF_V[n // 8])
                pe.wait_ge(att["ptc"], n + 1)
                if n % 4 == 0 and n >= 8:
                    pe.wait_ge(att["oc"], n // 4 - 1)
                b, c, n2 = bank[2 + n // 4 % 2], (n % 4) * P, n * HD
                mm(b[:, c:c + HD], pT[:, n % 2, 0:P], v[:, 0, n2:n2 + HD], start=True, stop=True)
                mm(b[:, c + HD:c + P], pT[:, n % 2, P:2 * P], v[:, 0, n2:n2 + HD], start=True, stop=False)
                mm(b[:, c + HD:c + P], pT[:, n % 2, 2 * P:3 * P], v[:, 1, n2:n2 + HD], start=False,
                   stop=True).then_inc(att["pv"], 1)

            for kind, n in ATT_ORDER:
                if kind == "project":
                    project(n)
                elif kind == "scores":
                    scores(n)
                elif kind == "turn":
                    turn(n)
                else:
                    values(n)
            pe.wait_ge(att["o"], TB)
            token_transposes(pe, osb, 4, att["oT"])
            pe.wait_ge(att["oTa"], 2)
            pe.wait_ge(att["oTv"], 2)
            for k in range(KD):
                j = J_ATT + 6 + k // 4
                if k % 4 == 0:
                    filled(pe, j, pairs0)
                for t in range(TB):
                    for c in range(2):
                        mm(bank[2 * t + c][:, :], oT[:, k, t * P:(t + 1) * P],
                           tall(j)[:, k % 4, c * 512:(c + 1) * 512], start=k == 0, stop=k == KD - 1,
                           skip_group_check=True)
                if k % 4 == 3:
                    pe.drain().then_inc(w_used, 1)
            pe.drain().then_inc(mix_mm, 1)
            normed(3)
            experts(1, J_MOE1, pairs0)

        @block.gpsimd
        def _(pool):
            T = nc.gpsimd.tensor_tensor
            pool.memset(minus_half, -0.5).then_inc(pool_c, 1)
            pool.wait_ge(pool_c, 1)
            for i in range(1, 24):
                if i % 3:
                    split_low(pool, nc.gpsimd, i, w_low_p)
                if i >= 20:
                    low_chunk(pool, J_Z, i - 20)
                if i == 10:
                    pool.wait_ge(tb_row, 1)
                    pool.dma_start(toeplitz_rows, trow[:, :]).then_inc(tb_out, 16)
            for g in range(G):
                heads = slice(g * HG, (g + 1) * HG)
                if g == 0:
                    pool.wait_ge(r_in, 16)
                pool.wait_ge(xt_ready, 4 * g + 4)
                pool.wait_ge(dt_c, 1)
                if g:
                    pool.wait_ge(st_mm, g)
                T(xw.rearrange("p (r c) -> p r c", r=HG), xtok[:, g, 0, :].rearrange("p (r c) -> p r c", r=HG),
                  dts[:, 7, 0, heads].unsqueeze(2).to_broadcast([P, HG, HD]), ALU.mult).then_inc(xw_ready, 1)
                if g:
                    pool.wait_ge(y_gated, g)
                for t in range(TB):
                    T(xd[:, t, :].rearrange("p (r c) -> p r c", r=HG),
                      xtok[:, g, t, :].rearrange("p (r c) -> p r c", r=HG),
                      row[:, R_DS + g * HG:R_DS + (g + 1) * HG].unsqueeze(2).to_broadcast([P, HG, HD]),
                      ALU.mult).then_inc(xd_ready, 1)
                for c in range(4):
                    low_chunk(pool, J_Z + 2 * (g + 1), c)
                st = stats[:, g * TB:(g + 1) * TB]
                pool.wait_ge(var_ready, g + 1)
                T(st, st, minus_half, ALU.pow).then_inc(rstd_ready, 1)
            for i in range(1, 4):
                for c in range(4):
                    low_chunk(pool, J_OUT + 2 * i, c)
            pool.wait_ge(tb_out, 16)
            pool.wait_ge(mix_mm, 1)
            skewed = bass.AP(tensor=toeplitz_rows.tensor, offset=toeplitz_rows.offset,
                             ap=[[1, P], [384, AH], [1, S]])
            pool.dma_start(bias[:, :, :], skewed).then_inc(tb_in, 16)
            for n, st in enumerate((lnst, lnst, lnst2, lnst)):
                for t in range(TB):
                    pool.wait_ge(var_ready, G + TB * n + t + 1)
                    rs = st[:, 28 + t:29 + t]
                    T(rs, rs, minus_half[:, 0:1], ALU.pow).then_inc(rstd_ready, 1)
                pool.wait_ge(ln_in, 32 * (n + 1))
                if n < 3:
                    pool.wait_ge(hT_mm, 4 * (n + 1))
                else:
                    pool.wait_ge(xn_ready, TB * 3 + 2)
                for t in range(TB):
                    if n < 3 or t == 1:
                        T(h[:, t, :], h[:, t, :], lnw[:, 0, :], ALU.mult).then_inc(pool_c, 1)
                        pool.wait_ge(pool_c, 2 + TB * n + (t if n < 3 else 0))
                        last = T(h[:, t, :], h[:, t, :], lnw[:, 1, :], ALU.add)
                last.then_inc(h_ready if n < 3 else h_final[1], 1)
                if n in (0, 2):
                    pool.memset(yacc[:, :, :], 0.0).then_inc(moe[n // 2]["added"], 1)

        @block.scalar
        def _(act):
            A = nc.scalar.activation
            link = in_order(act, act_c)
            act.dma_start(row[:, :], rows.partition_broadcast(P)).then_inc(r_in, 16)
            act.dma_start(bp[:, :], bias_pack).then_inc(b_in, 16)
            def load_ln(n):
                if n:
                    act.wait_ge(h_ready, n)
                for a, w in ((0, ln_g), (1, ln_b)):
                    act.dma_start(lnw[:, a, :], w[n // 2, n % 2].partition_broadcast(P)).then_inc(ln_in, 16)

            act.wait_ge(x_in, 16)
            A(xT_high, hT[:, :, :], ACT.Copy).then_inc(x_high, 1)

            def split_high(i):
                if i < 24:
                    if i % 4 == 0 or i == 1:
                        filled(act, J_IN + i // 4)
                    if i > NSPLIT:
                        act.wait_ge(ch_mm, i - NSPLIT + 1)
                    A(w_split[:, i % NSPLIT, 0], wide(J_IN + i // 4)[:, :, (i % 4) * P:(i % 4 + 1) * P],
                      ACT.Copy).then_inc(w_high, 1)

            for i in range(1, NSPLIT):
                split_high(i)
            act.wait_ge(c_in, 16)
            cw = lambda i, k: cst[:, C_CW + i * 4 + k:C_CW + i * 4 + k + 1]
            chan = [16 + i if i < 8 else i - 8 for i in range(24)]

            def seed(i):
                act.wait_ge(ch_mm, i + 1)
                if i >= 2:
                    act.wait_ge(ch_silu, i - 1)
                A(conv_acc[:, i % 2, :], bank[i % 2][:, 0:S], ACT.Identity, scale=cw(chan[i], 3),
                  bias=cst[:, C_CB + chan[i]:C_CB + chan[i] + 1]).then_inc(ch_seed, 1)

            def silu(i):
                act.wait_ge(ch_conv, i + 1)
                if i >= 10:
                    act.wait_ge(xt_mm, i - 9)
                dst = bcT[:, i, :] if i < 8 else xcm[:, i % 2, :]
                A(dst, conv_acc[:, i % 2, :], ACT.Silu).then_inc(ch_silu, 1)

            def xt_copy(i):
                act.wait_ge(xt_mm, i + 1)
                A(xtok[:, i // 4, :, i % 4 * P:(i % 4 + 1) * P], bank[4 + i % 2][:, 0:S].rearrange("p (t c) -> p t c", t=TB),
                  ACT.Copy).then_inc(xt_ready, 1)

            def dt_steps():
                act.wait_ge(dt_a, 1)
                A(dts[:, 1, :, :], dts[:, 1, :, :], ACT.Exp).then_inc(dt_b, 1)
                act.wait_ge(r_in, 16)
                A(dts[:, 9, 0, :], row[:, R_AL:R_AL + NH], ACT.Exp).then_inc(dt_b, 1)
                act.wait_ge(dt_b, 2)
                A(dts[:, 1, :, :], dts[:, 1, :, :], ACT.Ln, bias=1.0).then_inc(dt_b, 1)

            for i in range(24):
                if i:
                    silu(i - 1)
                if i >= 11:
                    xt_copy(i - 11)
                seed(i)
                split_high(i + NSPLIT)
                if 17 <= i < 21:
                    high_chunk(act, J_Z, i - 17)
                if i == 3:
                    dt_steps()
                if i == 10:
                    act.wait_ge(btok_mm, 1)
                    A(btok.rearrange("p g n -> p (g n)"), bank[6][:, :], ACT.Copy).then_inc(btok_ready, 1)
            silu(23)
            for i in range(13, 16):
                xt_copy(i)
            act.wait_ge(dt_dve, 1)
            A(dts[:, 5, :, :], dts[:, 3, :, :], ACT.Exp).then_inc(dt_b, 1)
            A(dts[:, 6, :, :], dts[:, 4, :, :], ACT.Exp).then_inc(dt_b, 1)
            def yT_copy(g, first_bank):
                act.wait_ge(yT_mm, g + 1)
                for i in range(4 * g, 4 * g + 4):
                    A(yT_high[:, i, :], bank[first_bank + (i % 4) // 2][:, (i % 2) * S:(i % 2 + 1) * S], ACT.Copy,
                      scale=cst[:, C_NW + i:C_NW + i + 1]).then_inc(yT_ready, 1)

            for g in range(G):
                act.wait_ge(dec_sub, g + 1)
                for c in range(TB):
                    A(dec[:, c, :, :], dec[:, c, :, :], ACT.Exp).then_inc(dec_exp, 1)
                for c in range(4):
                    high_chunk(act, J_Z + 2 * (g + 1), c)
                act.wait_ge(z_mm, g + 1)
                if g == G - 1:
                    act.dma_start(h[:, :, :], x[0].rearrange("(t p) d -> p t d", p=P)).then_inc(h_in, 16)
                    load_ln(0)
                if g >= 2:
                    act.wait_ge(y_gated, g - 1)
                for t in range(TB):
                    last = A(zs[:, g % 2, t, :], bank[2 + t][:, :], ACT.Silu)
                last.then_inc(z_ready, 1)
                act.wait_ge(st_mm, g + 1)
                if g:
                    act.wait_ge(yo_mm, g)
                A(stT[:, :], bank[4][:, :], ACT.Copy).then_inc(st_ready, 1)
                if g:
                    yT_copy(g - 1, 6)
                act.wait_ge(y_gated, g + 1)
                for t in range(TB):
                    if t or g:
                        act.wait_ge(y_sq, g * TB + t)
                    A(sq[:, :], y[:, g, t, :], ACT.Square,
                      accum_out=stats[:, g * TB + t:g * TB + t + 1]).then_inc(y_sq, 1)
            for i in range(1, 4):
                for c in range(4):
                    high_chunk(act, J_OUT + 2 * i, c)
            yT_copy(3, 0)

            def copy_hT(n):
                for i in (0, 2):
                    act.wait_ge(hT_mm, 4 * n + i + 1)
                    for k in (2 * i, 2 * i + 1):
                        g, b = C_LNG + n * KD + k, C_LNB + n * KD + k
                        last = A(hT[:, k, :], bank[4 + i][:, (k % 2) * S:(k % 2 + 1) * S], ACT.Identity,
                                 scale=cst[:, g:g + 1], bias=cst[:, b:b + 1])
                    last.then_inc(hT_a, 1)

            def copy_exT(m, n):
                act.wait_ge(m["gathered"], n)
                A(exT[:, 0:4, :], bank[0][:, :].rearrange("p (k c) -> p k c", k=4),
                  ACT.Copy).then_inc(m["exT_a"], 1)

            def expert_pair(m, q, following):
                act.wait_ge(m["gate"], q + 1)
                act.wait_ge(m["hid"], q + 1)
                A(silu_g[:, :], bank[2][:, :], ACT.Silu).then_inc(m["silu"], 1)
                if following:
                    copy_exT(m, q + 2)
                act.wait_ge(m["tr"], q + 1)
                act.wait_ge(m["added"], q * 4 + 1)
                A(selgT[:, :], bank[7][:, 0:S], ACT.Copy).then_inc(m["selgT"], 1)
                act.wait_ge(m["down"], q + 1)
                A(yex[:, 0:512], bank[5][:, :], ACT.Copy).then_inc(m["yex_a"], 1)

            def experts(L):
                m = moe[L]
                act.wait_ge(m["gsub"], 1)
                ge = rt[:, 64:72]
                A(ge, ge, ACT.Exp).then_inc(m["gexp"], 1)
                act.wait_ge(m["dsub"], 1)
                A(rt[:, 72:74], rt[:, 72:74], ACT.Exp).then_inc(m["dexp"], 1)
                copy_exT(m, 1)
                act.wait_ge(m["turned"], 1)
                A(tablesT, bank[6][:, :], ACT.Copy).then_inc(m["turnedc"], 1)
                act.wait_ge(m["route"], 1)
                further = further_pairs(act, L)
                with act.Fori(0, further) as q:
                    expert_pair(m, q, True)
                expert_pair(m, further, False)

            copy_hT(0)
            load_ln(1)
            experts(0)
            for i in range(8):
                act.wait_ge(att["rev"], i + 1)
                A(bias[:, 2 * i:2 * i + 2, :], bank[i % 2][:, :].rearrange("p (h c) -> p h c", h=2),
                  ACT.Copy).then_inc(att["bias"], 1)
            copy_hT(1)
            load_ln(2)
            def projected(u):
                act.wait_ge(att["proj"], u + 1)
                A(unit_buffer(u), bank[u % 2][:, 0:512 if UNITS[u][0] == "V" else S],
                  ACT.Copy).then_inc(att["ev_a"], 1)

            def probabilities(n):
                act.wait_ge(att["negmax"], n + 1)
                A(scb[:, n % 2, 0:P], scb[:, n % 2, 0:P], ACT.Exp, bias=am[:, 1, 0, n:n + 1],
                  accum_out=am[:, 2, 0, n:n + 1])
                A(scb[:, n % 2, P:384], scb[:, n % 2, P:384], ACT.Exp, bias=am[:, 1, 1, n:n + 1],
                  accum_out=am[:, 2, 1, n:n + 1]).then_inc(att["prob"], 1)

            def pt_copy(n):
                act.wait_ge(att["pt"], n + 1)
                if n >= 2:
                    act.wait_ge(att["pv"], n - 1)
                A(pT[:, n % 2, :], bank[6 + n % 2][:, 0:384], ACT.Copy).then_inc(att["ptc"], 1)

            def o_copy(n):
                act.wait_ge(att["pv"], n + 1)
                A(osb[:, :, (n - 3) * HD:(n + 1) * HD].rearrange("p t (j c) -> p j t c", j=4),
                  bank[2 + n // 4 % 2][:, :].rearrange("p (j t c) -> p j t c", j=4, t=TB),
                  ACT.Copy).then_inc(att["oc"], 1)

            for kind, n in ATT_ORDER:
                if kind == "project" and n % 2 == 0:
                    projected(n)
                elif kind == "scores":
                    probabilities(n)
                elif kind == "turn":
                    pt_copy(n)
                elif kind == "values" and n % 4 == 3:
                    o_copy(n)
            A(am[:, 3, :, :], am[:, 2, :, :], ACT.Ln).then_inc(att["ln"], 1)
            act.wait_ge(att["lse"], 1)
            A(am[:, 6, :, 0:3], am[:, 6, :, 0:3], ACT.Exp).then_inc(att["wexp"], 1)
            for i in (0, 2):
                act.wait_ge(att["oT"], i + 1)
                A(oT[:, 2 * i:2 * i + 2, :], bank[4 + i][:, :].rearrange("p (k s) -> p k s", k=2),
                  ACT.Copy).then_inc(att["oTa"], 1)
            copy_hT(2)
            load_ln(3)
            experts(1)

        @block.vector
        def _(dve):
            V = nc.vector
            link = in_order(dve, dve_c)
            cw = lambda i, k: cst[:, C_CW + i * 4 + k:C_CW + i * 4 + k + 1]
            chan = [16 + i if i < 8 else i - 8 for i in range(24)]
            def dt_steps():
                dve.wait_ge(dt_mm, 1)
                dve.wait_ge(r_in, 16)
                link(V.tensor_tensor(dts[:, 0, :, :], bank[6][:, 0:64].rearrange("p (t h) -> p t h", t=TB),
                                     row[:, R_DTB:R_DTB + NH].unsqueeze(1).to_broadcast([P, TB, NH]), ALU.add))
                link(V.tensor_scalar(dts[:, 2, :, :], dts[:, 0, :, :], -1.0, None, ALU.mult))
                V.tensor_tensor(dts[:, 1, :, :], dts[:, 0, :, :], dts[:, 2, :, :], ALU.min).then_inc(dt_a, 1)
                link(V.tensor_scalar(dts[:, 8, :, :], dts[:, 0, :, :], 0.0, None, ALU.max))
                dve.wait_ge(dt_b, 3)
                link(V.tensor_tensor(dts[:, 8, :, :], dts[:, 8, :, :], dts[:, 1, :, :], ALU.add))
                V.scalar_tensor_tensor(dts[:, 2, :, :], dts[:, 8, :, :], -1.0,
                                       dts[:, 9, 0:1, :].to_broadcast([P, TB, NH]), ALU.mult,
                                       ALU.mult).then_inc(dt_ready, 1)
                dve.wait_ge(tb_mm, 1)
                V.tensor_tensor(trow[:, :], bank[7][0:AH, 0:384], bp[0:AH, 384:768], ALU.add).then_inc(tb_row, 1)

            dve.wait_ge(x_high, 1)
            V.tensor_tensor(xT_low, hT[:, :, :], xT_high, ALU.subtract).then_inc(x_low, 1)
            for i in range(24):
                if i == 3:
                    dt_steps()
                dve.wait_ge(ch_seed, i + 1)
                for s in (1, 2, 3):
                    ins = V.scalar_tensor_tensor(conv_acc[:, i % 2, s:S], bank[i % 2][:, 0:S - s],
                                                 cw(chan[i], 3 - s), conv_acc[:, i % 2, s:S], ALU.mult, ALU.add)
                    if s < 3:
                        link(ins)
                    else:
                        ins.then_inc(ch_conv, 1)
                if i % 3 == 0 and i + 3 < 24:
                    split_low(dve, V, i + 3, w_low_v)
                if i == 8:
                    dve.wait_ge(acs_mm, 1)
                    acs_ps = bank[7][:, 0:64].rearrange("p (t h) -> p t h", t=TB)
                    link(V.tensor_copy(dts[:, 3, :, :], acs_ps))
                    V.tensor_tensor(dts[:, 4, 0, :], bank[7][:, 64:96], dts[:, 3, 0, :], ALU.subtract)
                    V.tensor_copy(dts[:, 4, 1, :], dts[:, 3, 1, :]).then_inc(dt_dve, 1)
                if i == 9:
                    dve.wait_ge(cb_mm, 1)
                    for c in range(TB):
                        ins = V.tensor_tensor(cbm[:, c, :, :], bank[4 + c][:, :].rearrange("p (g i) -> p g i", g=G),
                                              tri.unsqueeze(1).to_broadcast([P, G, P]), ALU.mult)
                    ins.then_inc(cb_ready, 1)
            dve.wait_ge(dt_b, 5)
            V.tensor_tensor(dts[:, 7, 0, :], dts[:, 6, 0, :], dts[:, 8, 0, :], ALU.mult).then_inc(dt_c, 1)
            dve.wait_ge(tb_out, 16)

            def yT_split(g, first_bank):
                for i in range(4 * g, 4 * g + 4):
                    if i % 2 == 0:
                        dve.wait_ge(yT_ready, i + 2)
                    V.scalar_tensor_tensor(yT_low[:, i, :], bank[first_bank + (i % 4) // 2][:, (i % 2) * S:(i % 2 + 1) * S],
                                           cst[:, C_NW + i:C_NW + i + 1], yT_high[:, i, :], ALU.mult,
                                           ALU.subtract).then_inc(yT_rest, 1)

            for g in range(G):
                dve.wait_ge(dec_mm, g + 1)
                if g:
                    dve.wait_ge(yd_mm, g)
                for c in range(TB):
                    for r in range(HG):
                        hh = g * HG + r
                        ins = V.tensor_scalar(dec[:, c, r, :], bank[4 + 2 * c + r // 4][:, (r % 4) * P:(r % 4 + 1) * P],
                                              dts[:, 3, c, hh:hh + 1], 0.0, ALU.subtract, ALU.min)
                ins.then_inc(dec_sub, 1)
                for c in range(TB):
                    dve.wait_ge(dec_exp, g * TB + c + 1)
                    for r in range(HG):
                        hh = g * HG + r
                        ins = V.scalar_tensor_tensor(dec[:, c, r, :], dec[:, c, r, :], dts[:, 8, c, hh:hh + 1],
                                                     cbm[:, c, g, :], ALU.mult, ALU.mult)
                ins.then_inc(dec_ready, 1)
                if g:
                    yT_split(g - 1, 6)
                dve.wait_ge(yd_mm, g + 1)
                dve.wait_ge(xd_ready, TB * (g + 1))
                for t in range(TB):
                    link(V.tensor_tensor(y[:, g, t, :], bank[t][:, :], xd[:, t, :], ALU.add))
                dve.wait_ge(yo_mm, g + 1)
                ea = dts[:, 5, 1, g * HG:(g + 1) * HG].unsqueeze(2).to_broadcast([P, HG, HD])
                link(V.tensor_tensor(xd[:, 1, :].rearrange("p (r c) -> p r c", r=HG),
                                     bank[3][:, :].rearrange("p (r c) -> p r c", r=HG), ea, ALU.mult))
                link(V.tensor_tensor(y[:, g, 1, :], y[:, g, 1, :], xd[:, 1, :], ALU.add))
                dve.wait_ge(z_ready, g + 1)
                V.tensor_tensor(y[:, g, :, :], y[:, g, :, :], zs[:, g % 2, :, :], ALU.mult).then_inc(y_gated, 1)
                dve.wait_ge(y_sq, TB * (g + 1))
                st = stats[:, g * TB:(g + 1) * TB]
                V.tensor_scalar(st, st, 1.0 / 512, EPS, ALU.mult, ALU.add).then_inc(var_ready, 1)
                dve.wait_ge(rstd_ready, g + 1)
                for t in range(TB):
                    ins = V.tensor_scalar(y[:, g, t, :], y[:, g, t, :], st[:, t:t + 1], None, ALU.mult)
                ins.then_inc(y_ready, 1)
            yT_split(3, 0)

            def layer_norm(n, mix, st):
                if n:
                    dve.wait_ge(h_ready, n)
                sums = st[:, 0:24].rearrange("p (t c s) -> p t c s", t=TB, c=2)
                mv = st[:, 24:28].rearrange("p (t s) -> p t s", t=TB)
                rs = st[:, 28:30]
                for t in range(TB):
                    for c in range(2):
                        cc = slice(c * 512, (c + 1) * 512)
                        link(V.scalar_tensor_tensor(h[:, t, cc], h[:, t, cc], ALPHA, mix(t, c), ALU.mult, ALU.add))
                for t in range(TB):
                    for c in range(2):
                        link(V.bn_stats(sums[:, t, c, :], h[:, t, c * 512:(c + 1) * 512]))
                    link(V.bn_aggr(mv[:, t, :], sums[:, t, :, :].rearrange("p c s -> p (c s)")))
                    V.tensor_scalar(rs[:, t:t + 1], mv[:, t, 1:2], EPS, None, ALU.add).then_inc(var_ready, 1)
                for t in range(TB):
                    dve.wait_ge(rstd_ready, G + TB * n + t + 1)
                    V.tensor_scalar(h[:, t, :], h[:, t, :], mv[:, t, 0:1], rs[:, t:t + 1],
                                    ALU.subtract, ALU.mult).then_inc(xn_ready, 1)
                if n == 3:
                    dve.wait_ge(xn_ready, TB * 3 + 1)
                    dve.wait_ge(ln_in, 32 * 4)
                    link(V.tensor_tensor(h[:, 0, :], h[:, 0, :], lnw[:, 0, :], ALU.mult))
                    V.tensor_tensor(h[:, 0, :], h[:, 0, :], lnw[:, 1, :], ALU.add).then_inc(h_final[0], 1)

            def copy_hT(n):
                for i in (1, 3):
                    dve.wait_ge(hT_mm, 4 * n + i + 1)
                    for k in (2 * i, 2 * i + 1):
                        g, b = C_LNG + n * KD + k, C_LNB + n * KD + k
                        last = V.tensor_scalar(hT[:, k, :], bank[4 + i][:, (k % 2) * S:(k % 2 + 1) * S],
                                               cst[:, g:g + 1], cst[:, b:b + 1], ALU.mult, ALU.add)
                    last.then_inc(hT_v, 1)

            def slots(n):
                return iota.unsqueeze(1).unsqueeze(1).to_broadcast([P, TB, n, CAP])

            def of_pair(table, q):
                return table[:, :, bass.ds(q * 2, 2)].unsqueeze(3).to_broadcast([P, TB, 2, CAP])

            def select(m, r):
                V.tensor_tensor(sel.rearrange("p t (e c) -> p t e c", e=2), slots(2), r,
                                ALU.is_equal).then_inc(m["sel"], 1)

            def select_gated(m, q):
                sg = selg.rearrange("p t (e c) -> p t e c", e=2)
                V.tensor_tensor(sg, slots(2), of_pair(rank_item, q), ALU.is_equal).then_inc(m["end"], 1)
                dve.wait_ge(m["end"], q + 1)
                V.tensor_tensor(sg, sg, of_pair(gate_item, q), ALU.mult)

            def copy_exT(m, n):
                dve.wait_ge(m["gathered"], n)
                V.tensor_copy(exT[:, 4:8, :], bank[1][:, :].rearrange("p (k c) -> p k c", k=4)
                              ).then_inc(m["exT_v"], 1)

            def expert_pair(m, q, following):
                dve.wait_ge(m["silu"], q + 1)
                dve.wait_ge(m["up"], q + 1)
                V.tensor_tensor(hid[:, :], silu_g[:, :], bank[3][:, :], ALU.mult).then_inc(m["hid"], 1)
                if following:
                    copy_exT(m, q + 2)
                dve.wait_ge(m["tr"], q + 1)
                V.tensor_copy(hidT.rearrange("p k c -> p (k c)"), bank[4][:, :]).then_inc(m["hidT"], 1)
                if following:
                    select_gated(m, q + 1)
                    select(m, of_pair(rank_item, q + 2))
                dve.wait_ge(m["down"], q + 1)
                V.tensor_copy(yex[:, 512:1024], bank[6][:, :]).then_inc(m["yex_v"], 1)
                for i, (t, c) in enumerate(((0, 0), (0, 1), (1, 0), (1, 1))):
                    dve.wait_ge(m["comb"], q * 4 + (i + 1))
                    a = yacc[:, t, c * 512:(c + 1) * 512]
                    V.tensor_tensor(a, a, bank[7 if i % 2 == 0 else 4][:, :], ALU.add).then_inc(m["added"], 1)

            def experts(L):
                m = moe[L]
                T = V.tensor_tensor
                r3 = lambda a, n, w: rt[:, a:a + 2 * n].rearrange("p (t e) -> p t e", t=TB)
                mask = r3(0, E, 0)
                ge = r3(64, 4, 0)
                dd = rt[:, 72:74].rearrange("p (t e) -> p t e", t=TB)
                lg = r3(80, 36, 0)
                gpad = r3(152, 8, 0)
                gtop = r3(168, 8, 0)
                goh = r3(184, 4, 0)
                gval = r3(192, 1, 0)
                sl = r3(200, 8, 0)
                etop = r3(216, 8, 0)
                fi = r3(232, 8, 0)
                oh0 = r3(248, 8, 0)
                oh1 = r3(264, 8, 0)
                pr = r3(280, 2, 0)
                rr = r3(284, 1, 0)
                gt = r3(300, E, 0)
                cnt = rt[:, 370:380]
                tmp = rt[:, 400:464].rearrange("p (t g e) -> p t g e", t=TB, g=G)
                link(V.memset(gpad, -3.0e38))
                V.memset(cnt[:, 9:10], 0.0).then_inc(m["hid"], 1)
                dve.wait_ge(m["logit"], 1)
                c = R_RB + L * 36
                link(T(lg, bank[0][:, 0:72].rearrange("p (t e) -> p t e", t=TB),
                       row[:, c:c + 36].unsqueeze(1).to_broadcast([P, TB, 36]), ALU.add))
                link(V.tensor_copy(gpad[:, :, 0:4], lg[:, :, 0:4]))
                ix = idx[:, 0:16].rearrange("p (t e) -> p t e", t=TB)
                for t in range(TB):
                    link(V.max(gtop[:, t, :], gpad[:, t, :]))
                    link(V.max_index(ix[:, t, :], gtop[:, t, :], gpad[:, t, :]))
                T(ge, lg[:, :, 0:4], gtop[:, :, 0:1].to_broadcast([P, TB, 4]), ALU.subtract).then_inc(m["gsub"], 1)
                link(V.tensor_scalar(fi, ix, 1.0, None, ALU.add))
                link(T(goh, iota[:, 0:4].unsqueeze(1).to_broadcast([P, TB, 4]),
                       fi[:, :, 0:1].to_broadcast([P, TB, 4]), ALU.is_equal))
                link(T(tmp, lg[:, :, 4:36].rearrange("p t (g e) -> p t g e", g=G),
                       goh.unsqueeze(3).to_broadcast([P, TB, G, 8]), ALU.mult))
                link(V.tensor_reduce(sl, tmp.rearrange("p t g e -> p t e g"), AX.X, ALU.add))
                for t in range(TB):
                    link(V.max(etop[:, t, :], sl[:, t, :]))
                    link(V.max_index(ix[:, t, :], etop[:, t, :], sl[:, t, :]))
                T(dd, etop[:, :, 1:2], etop[:, :, 0:1], ALU.subtract).then_inc(m["dsub"], 1)
                link(V.tensor_scalar(fi, ix, 1.0, None, ALU.add))
                i8 = iota[:, 0:8].unsqueeze(1).to_broadcast([P, TB, 8])
                link(T(oh0, i8, fi[:, :, 0:1].to_broadcast([P, TB, 8]), ALU.is_equal))
                link(T(oh1, i8, fi[:, :, 1:2].to_broadcast([P, TB, 8]), ALU.is_equal))
                link(T(sl, oh0, oh1, ALU.add))
                T(mask.rearrange("p t (g e) -> p t g e", g=G), goh.unsqueeze(3).to_broadcast([P, TB, G, 8]),
                  sl.unsqueeze(2).to_broadcast([P, TB, G, 8]), ALU.mult).then_inc(m["mask"], 1)
                dve.wait_ge(m["rank"], 1)
                link(T(gt, bank[4][:, 0:2 * E].rearrange("p (t e) -> p t e", t=TB), mask, ALU.mult))
                link(T(gt, gt, mask, ALU.add))
                select(m, gt[:, :, 0:2].unsqueeze(3).to_broadcast([P, TB, 2, CAP]))
                active = rt[:, 380:381]
                T(active, bank[4][:, 2 * E:2 * E + 1], cst[:, C_THR:C_THR + 1], ALU.is_gt).then_inc(m["active"], 1)
                for b in range(NBLK):
                    V.tensor_scalar(tables[:, 0, :, b * E:(b + 1) * E], gt, -1.0 * CAP * b, None, ALU.add)
                dve.wait_ge(m["gexp"], 1)
                link(V.tensor_reduce(gval, ge, AX.X, ALU.add))
                dve.wait_ge(m["dexp"], 1)
                link(V.tensor_scalar(rr, dd, 1.0, None, ALU.add))
                link(T(rr, rr, gval, ALU.mult))
                link(V.reciprocal(pr[:, :, 0:1], rr))
                link(T(pr[:, :, 1:2], pr[:, :, 0:1], dd, ALU.mult))
                link(T(oh0, oh0, pr[:, :, 0:1].to_broadcast([P, TB, 8]), ALU.mult))
                link(T(oh1, oh1, pr[:, :, 1:2].to_broadcast([P, TB, 8]), ALU.mult))
                link(T(oh0, oh0, oh1, ALU.add))
                for b in range(NBLK):
                    ins = T(tables[:, 1, :, b * E:(b + 1) * E].rearrange("p t (g e) -> p t g e", g=G),
                            goh.unsqueeze(3).to_broadcast([P, TB, G, 8]),
                            oh0.unsqueeze(2).to_broadcast([P, TB, G, 8]), ALU.mult)
                ins.then_inc(m["table"], 1)
                dve.wait_ge(m["place"], 1)
                link(T(cnt[:, 0:1], bank[5][:, 0:1], active, ALU.mult))
                link(T(cnt[:, 1:2], cnt[:, 0:1], active, ALU.add))
                T(is_item, iota[:, 0:NITEM], cnt[:, 1:2].to_broadcast([P, NITEM]), ALU.is_equal).then_inc(m["item"], 1)
                copy_exT(m, 1)
                dve.wait_ge(m["listed"], 1)
                link(V.tensor_copy(small[0:1, L, 0:NITEM], bank[5][0:1, 64:64 + NITEM]))
                taken = bank[5][0:1, 130:128 + NITEM].rearrange("p (i two) -> p i two", two=2)
                link(V.tensor_reduce(cnt[0:1, 5:6], taken[:, :, 0], AX.X, ALU.add))
                link(V.tensor_copy(small[0:1, L, NITEM:NITEM + 1], cnt[0:1, 5:6]))
                V.tensor_copy(cnt[:, 6:7], cnt[:, 0:1]).then_inc(m["route"], 1)
                n = TB * NITEM
                link(V.tensor_copy(rank_item.rearrange("p t i -> p (t i)"), bank[7][:, 0:n]))
                link(V.tensor_copy(gate_item.rearrange("p t i -> p (t i)"), bank[7][:, n:2 * n]))
                dve.wait_ge(m["route"], 1)
                further = further_pairs(dve, L)
                select_gated(m, 0)
                select(m, of_pair(rank_item, 1))
                with dve.Fori(0, further) as q:
                    expert_pair(m, q, True)
                expert_pair(m, further, False)
                dve.wait_ge(m["added"], further * 4 + 5)

            dve.wait_ge(h_in, 16)
            dve.wait_ge(mix_mm, 1)
            layer_norm(0, lambda t, c: bank[4 + 2 * t + c][:, :], lnst)
            copy_hT(0)
            experts(0)
            layer_norm(1, lambda t, c: yacc[:, t, c * 512:(c + 1) * 512], lnst)
            copy_hT(1)
            def projected(u):
                dve.wait_ge(att["proj"], u + 1)
                V.tensor_copy(unit_buffer(u), bank[u % 2][:, 0:512 if UNITS[u][0] == "V" else S]
                              ).then_inc(att["ev_v"], 1)

            def logits(n):
                dve.wait_ge(att["score"], n + 1)
                if n >= 2:
                    dve.wait_ge(att["pt"], n - 1)
                s = scb[:, n % 2, :]
                V.scalar_tensor_tensor(s[:, 0:P], bank[4 + n % 2][:, 0:P], SCALE, bias[:, n, P:S],
                                       ALU.mult, ALU.add)
                link(V.scalar_tensor_tensor(s[:, P:384], bank[4 + n % 2][:, P:384], SCALE, bias[:, n, :],
                                            ALU.mult, ALU.add))
                V.tensor_reduce(am[:, 0, 0, n:n + 1], s[:, 0:P], AX.X, ALU.max)
                link(V.tensor_reduce(am[:, 0, 1, n:n + 1], s[:, P:384], AX.X, ALU.max))
                V.tensor_scalar(am[:, 1, :, n:n + 1], am[:, 0, :, n:n + 1], -1.0, None,
                                ALU.mult).then_inc(att["negmax"], 1)

            dve.wait_ge(att["bias"], 8)
            for kind, n in ATT_ORDER:
                if kind == "project" and n % 2 == 1:
                    projected(n)
                elif kind == "scores":
                    logits(n)
            dve.wait_ge(att["ln"], 1)
            link(V.tensor_tensor(am[:, 4, :, :], am[:, 3, :, :], am[:, 0, :, :], ALU.add))
            for i, (a, n) in enumerate(AGROUPS):
                link(V.tensor_reduce(am[:, 5, :, i:i + 1], am[:, 4, :, a:a + n], AX.X, ALU.add))
                link(V.tensor_scalar(am[:, 5, :, i:i + 1], am[:, 5, :, i:i + 1], 1.0 / n, None, ALU.mult))
            link(V.tensor_reduce(am[:, 7, :, 0:1], am[:, 5, :, 0:3], AX.X, ALU.max))
            V.tensor_tensor(am[:, 6, :, 0:3], am[:, 5, :, 0:3], am[:, 7, :, 0:1].to_broadcast([P, TB, 3]),
                            ALU.subtract).then_inc(att["lse"], 1)
            dve.wait_ge(att["wexp"], 1)
            link(V.tensor_reduce(am[:, 7, :, 1:2], am[:, 6, :, 0:3], AX.X, ALU.add))
            link(V.reciprocal(am[:, 7, :, 2:3], am[:, 7, :, 1:2]))
            link(V.tensor_scalar(am[:, 7, :, 2:3], am[:, 7, :, 2:3], 3.0, None, ALU.mult))
            link(V.tensor_tensor(am[:, 6, :, 0:3], am[:, 6, :, 0:3], am[:, 7, :, 2:3].to_broadcast([P, TB, 3]),
                                 ALU.mult))
            link(V.reciprocal(am[:, 8, :, :], am[:, 2, :, :]))
            for i, (a, n) in enumerate(AGROUPS):
                link(V.tensor_tensor(am[:, 8, :, a:a + n], am[:, 8, :, a:a + n],
                                     am[:, 6, :, i:i + 1].to_broadcast([P, TB, n]), ALU.mult))
            dve.wait_ge(att["oc"], 4)
            for t in range(TB):
                o4 = osb[:, t, :].rearrange("p (r c) -> p r c", r=AH)
                V.tensor_tensor(o4, o4, am[:, 8, t, :].unsqueeze(2).to_broadcast([P, AH, HD]),
                                ALU.mult).then_inc(att["o"], 1)
            for i in (1, 3):
                dve.wait_ge(att["oT"], i + 1)
                V.tensor_copy(oT[:, 2 * i:2 * i + 2, :],
                              bank[4 + i][:, :].rearrange("p (k s) -> p k s", k=2)).then_inc(att["oTv"], 1)
            dve.wait_ge(mix_mm, 2)
            layer_norm(2, lambda t, c: bank[2 * t + c][:, :], lnst2)
            copy_hT(2)
            experts(1)
            layer_norm(3, lambda t, c: yacc[:, t, c * 512:(c + 1) * 512], lnst)


UNITS = [("K", i, J_ATT, i == 0, i == 3) for i in range(4)]
UNITS += [("Q", i, J_ATT + 1, i == 0, i == 3) for i in range(4)]
UNITS += [("V", i, J_ATT + 2 + i // 2, i % 2 == 0, i % 2 == 1) for i in range(4)]
for _i in range(4, 8):
    UNITS += [("K", _i, J_ATT + 4, _i == 4, _i == 7), ("Q", _i, J_ATT + 5, _i == 4, _i == 7)]
UNIT_OF_HEADS = [4 + i if i < 4 else 13 + 2 * (i - 4) for i in range(8)]
UNIT_OF_V = [9, 11]


def attention_order():
    order = [("project", u) for u in range(8)] + [("scores", 0), ("scores", 1)]

    def head(n):
        steps = [("turn", n)] if n < AH else []
        steps += [("scores", n + 2)] if n + 2 < AH else []
        return steps + ([("values", n - 1)] if n else [])

    n = 0
    for u in range(8, 20):
        order.append(("project", u))
        for _ in range(2 if u == 10 else 1):
            order += head(n)
            n += 1
    while n <= AH:
        order += head(n)
        n += 1
    return order


ATT_ORDER = attention_order()


def distances():
    y = np.arange(384)
    dist = 255 - y
    n = np.maximum(dist, 1).astype(np.float64)
    large = 16 + (np.log(n / 16) / np.log(2048 / 16) * 16).astype(np.int32)
    bucket = np.where(dist < 16, np.maximum(dist, 0), np.minimum(large, 31))
    onehot = (np.arange(32)[:, None] == bucket[None]).astype(np.float32)
    dil = np.array([1] * 6 + [4] * 5 + [16] * 5)[:, None]
    ok = (dist[None] >= 0) & (dist[None] % dil == 0) & (dist[None] // dil <= 128)
    return onehot, np.where(ok, 0.0, -1.0e30).astype(np.float32)


def kernel(**inputs):
    import concourse.bacc as bacc
    from concourse.bass_utils import run_bass_kernel_spmd as run

    a = {k: np.asarray(v) for k, v in inputs.items()}
    f = np.float32
    ca = np.ascontiguousarray
    lay = lambda w: w.reshape(KD, P, -1).transpose(1, 0, 2).reshape(P, -1)
    k = np.arange(P)
    router = [np.concatenate([a["moe_group_w"][i], a["moe_expert_w"][i].transpose(1, 0, 2).reshape(D, E)], 1)
              for i in range(2)]
    consts = np.concatenate([
        a["ssm_conv_w"][0].reshape(4, 24, P).transpose(2, 1, 0).reshape(P, 96),
        a["ssm_conv_b"][0].reshape(24, P).T,
        a["ssm_norm_w"][0].reshape(16, P).T,
        np.eye(P, dtype=f), (k[:, None] <= k[None]).astype(f), (k[:, None] < k[None]).astype(f),
        np.ones((P, P), f), np.broadcast_to(np.arange(1, CAP + 1, dtype=f), (P, CAP)),
        lay(router[0]), lay(router[1]), lay(a["ssm_in_w"][0][:, 5120:5152]),
        np.eye(P, dtype=f)[::-1], a["ln_g"].reshape(4 * KD, P).T, a["ln_b"].reshape(4 * KD, P).T,
        (k % E).astype(f)[:, None], np.where(k < 2, -1.0, k // E * CAP + 0.5).astype(f)[:, None]], 1)
    rows = np.concatenate([a["ssm_dt_bias"][0], a["ssm_a_log"][0], a["ssm_d"][0]]
                          + [b for i in range(2) for b in (a["moe_group_b"][i], a["moe_expert_b"][i].reshape(-1))])
    onehot, forbidden = distances()
    bias_pack = np.zeros((32, 784), f)
    bias_pack[:, 0:384] = onehot
    bias_pack[0:AH, 384:768] = forbidden
    bias_pack[:, 768:784] = a["rel_bias"]
    arrays = {
        "x": ca(a["x"]), "xT": ca(a["x"][0].T.reshape(KD, P, S).transpose(1, 0, 2)),
        "consts": ca(consts), "rows": ca(rows), "in_w": ca(a["ssm_in_w"][0]), "out_w": ca(a["ssm_out_w"][0]),
        "kv_w": ca(a["kv_w"]), "q_w": ca(a["attn_q_w"][0]), "o_w": ca(a["attn_o_w"][0]), "bias_pack": bias_pack,
        "gate_w": ca(a["moe_gate_w"].reshape(2, E, D, 512)), "up_w": ca(a["moe_up_w"].reshape(2, E, D, 512)),
        "down_w": ca(a["moe_down_w"].reshape(2, E, 512, D)), "ln_g": ca(a["ln_g"]), "ln_b": ca(a["ln_b"]),
    }
    nc = bacc.Bacc("TRN2", target_bir_lowering=False, num_devices=1)
    args = [nc.dram_tensor("in_" + n, v.shape, F32, kind="ExternalInput").ap() for n, v in arrays.items()]
    args.append(nc.dram_tensor("out_0", (1, S, D), F32, kind="ExternalOutput").ap())
    program(nc, *args)
    r = run(nc, [{"in_" + n: v for n, v in arrays.items()}], core_ids=[0])
    return r.results[0]["out_0"]
```

```python
import numpy as np
import concourse.bass as bass
from concourse import mybir
from contextlib import ExitStack

F32 = mybir.dt.float32
F32R = mybir.dt.float32r
ALU = mybir.AluOpType
ACT = mybir.ActivationFunctionType
AX = mybir.AxisListType

P = 128
D = 1024
S = 256
TB = S // P
KD = D // P
DI = 2048
NH = 32
HD = 64
G = 4
HG = NH // G
AH = 16
AGROUPS = ((0, 6), (6, 5), (11, 5))
E = 32
CAP = 64
NBLK = S // CAP
CAND = E * NBLK
NITEM = 44
assert CAND == P and NITEM >= E + (2 * S - E) // CAP + 5
RING = 6
SLOT = 4096
NSPLIT = 3
ALPHA = 4.0 ** 0.25
EPS = 1e-5
SCALE = HD ** -0.5

J_IN = 0
J_Z = J_IN + 6
J_OUT = J_Z + 8
J_MOE0 = J_OUT + 8
J_ATT = J_MOE0
J_MOE1 = J_ATT + 16

C_CW, C_CB, C_NW = 0, 96, 120
C_ID, C_TRI, C_STRI, C_ONE, C_IOTA = 136, 264, 392, 520, 648
C_RW = C_IOTA + 64
C_DTW = C_RW + 2 * KD * 36
C_REV = C_DTW + KD * NH
C_LNG = C_REV + P
C_LNB = C_LNG + 4 * KD
C_EXP = C_LNB + 4 * KD
C_THR = C_EXP + 1
C_END = C_THR + 1
R_DTB, R_AL, R_DS, R_RB = 0, 32, 64, 96
R_END = R_RB + 72


def program(nc, x, xT, consts, rows, in_w, out_w, kv_w, q_w, o_w, bias_pack, gate_w, up_w, down_w,
            ln_g, ln_b, out):
    ctx = ExitStack()
    with ctx:
        def sem(name):
            return ctx.enter_context(nc.semaphore(name))

        arena_words = 28400
        with nc.sbuf_tensor("split_ring", [P, RING, SLOT], F32R) as split_ring:
            pass
        ring = ctx.enter_context(nc.sbuf_tensor("ring", [P, RING, SLOT], F32))
        with nc.sbuf_tensor("split_arena", [P, arena_words], F32R) as split_arena:
            pass
        arena = ctx.enter_context(nc.sbuf_tensor("arena", [P, arena_words], F32))
        toeplitz_rows = nc.dram_tensor("toeplitz_rows", (AH, 384), F32).ap()
        bank = [ctx.enter_context(nc.psum_tensor(f"bank{i}", [P, 512], F32)) for i in range(8)]
        top = [0]

        def take(n):
            v = arena[:, top[0]:top[0] + n]
            top[0] += n
            assert top[0] <= arena_words
            return v

        cst = take(C_END)
        row = take(R_END)
        h_at = top[0]
        h = take(TB * D).rearrange("p (t d) -> p t d", t=TB)
        hT_at = top[0]
        hT = take(KD * S).rearrange("p (k s) -> p k s", k=KD)
        lnw_at = top[0]
        lnw = take(2 * D).rearrange("p (a d) -> p a d", a=2)
        ident = cst[:, C_ID:C_ID + P]
        tri = cst[:, C_TRI:C_TRI + P]
        stri = cst[:, C_STRI:C_STRI + P]
        ones = cst[:, C_ONE:C_ONE + P]
        iota = cst[:, C_IOTA:C_IOTA + CAP]
        minus_half = take(TB)
        work = top[0]

        xtok_f = take(TB * DI)
        xtok = xtok_f.rearrange("p (g t c) -> p g t c", g=G, t=TB)
        y_at = top[0]
        y = take(TB * DI).rearrange("p (g t c) -> p g t c", g=G, t=TB)
        zs = take(2 * TB * 512).rearrange("p (b t c) -> p b t c", b=2, t=TB)
        bcT = take(8 * S).rearrange("p (k s) -> p k s", k=8)
        cbm = take(TB * G * P).rearrange("p (c g i) -> p c g i", c=TB, g=G)
        dec = take(2 * HG * P).rearrange("p (c r i) -> p c r i", c=2, r=HG)
        btok = take(G * P).rearrange("p (g n) -> p g n", g=G)
        xw = take(512)
        xd = take(TB * 512).rearrange("p (t c) -> p t c", t=TB)
        stT = take(512)
        conv_acc = take(2 * S).rearrange("p (b s) -> p b s", b=2)
        xcm = take(2 * S).rearrange("p (b s) -> p b s", b=2)
        dts = take(10 * TB * NH).rearrange("p (a t h) -> p a t h", a=10, t=TB)
        sq = take(512)
        stats = take(64)

        yT_high = split_arena[:, work:work + TB * DI].rearrange("p (k s) -> p k s", s=S)
        yT_low = split_arena[:, y_at:y_at + TB * DI].rearrange("p (k s) -> p k s", s=S)
        xT_high = split_arena[:, h_at:h_at + KD * S].rearrange("p (k s) -> p k s", k=KD)
        xT_low = split_arena[:, lnw_at:lnw_at + KD * S].rearrange("p (k s) -> p k s", k=KD)
        w_split = split_arena[:, y_at:y_at + NSPLIT * 2 * D].rearrange("p (b a k c) -> p b a k c",
                                                                       b=NSPLIT, a=2, k=KD)

        top[0] = work
        sel = take(TB * P).rearrange("p (t c) -> p t c", t=TB)
        selg = take(TB * P).rearrange("p (t c) -> p t c", t=TB)
        exT = take(KD * P).rearrange("p (k c) -> p k c", k=KD)
        silu_g = take(512)
        hid = take(512)
        hidT = take(512).rearrange("p (k c) -> p k c", k=4)
        selgT = take(S)
        yex = take(D)
        yacc = take(TB * D).rearrange("p (t d) -> p t d", t=TB)
        rank_item = take(TB * NITEM).rearrange("p (t i) -> p t i", t=TB)
        gate_item = take(TB * NITEM).rearrange("p (t i) -> p t i", t=TB)
        tables = take(2 * TB * CAND).rearrange("p (a t c) -> p a t c", a=2, t=TB)
        tablesT = take(2 * TB * P)
        is_item = take(NITEM)
        rt = take(1400)
        lnst = take(64)
        after_moe = top[0]
        moe_top = top[0]

        top[0] = arena_words - 4096
        bias = take(AH * S).rearrange("p (h c) -> p h c", h=AH)
        top[0] = work
        qT = take(KD * S).rearrange("p (k s) -> p k s", k=KD)
        kT_at = top[0]
        kT = take(KD * S).rearrange("p (k s) -> p k s", k=KD)
        v = take(TB * D).rearrange("p (t d) -> p t d", t=TB)
        osb = take(TB * D).rearrange("p (t d) -> p t d", t=TB)
        oT_at = top[0]
        take(KD * S)
        scb = take(2 * 384).rearrange("p (b c) -> p b c", b=2)
        pT = take(2 * 384).rearrange("p (b c) -> p b c", b=2)
        am = take(12 * 32).rearrange("p (a q h) -> p a q h", a=12, q=2)
        lnst2 = take(64)
        aT_high = split_arena[:, top[0]:top[0] + KD * S].rearrange("p (k s) -> p k s", k=KD)
        take(KD * S)
        aT_low = split_arena[:, hT_at:hT_at + KD * S].rearrange("p (k s) -> p k s", k=KD)
        oT_high = split_arena[:, oT_at:oT_at + KD * S].rearrange("p (k s) -> p k s", k=KD)
        oT_low = split_arena[:, kT_at:kT_at + KD * S].rearrange("p (k s) -> p k s", k=KD)
        assert top[0] <= arena_words - 4096 and moe_top <= arena_words - 4096
        small = ctx.enter_context(nc.sbuf_tensor("small", [P, 2, NITEM + 1], mybir.dt.int32))
        idx = ctx.enter_context(nc.sbuf_tensor("idx", [P, 32], mybir.dt.uint32))
        dec_flat = dec.rearrange("p c r i -> p (c r i)")
        bp = dec_flat[0:32, 0:384 * 2 + AH]
        trow = dec_flat[0:AH, 1024:1024 + 384]

        w_full = [sem(f"w_full{i}") for i in range(RING)]
        piece_low = sem("piece_low")
        w_used = sem("w_used")
        x_in, c_in, r_in, h_in, b_in = (sem(n) for n in ("x_in", "c_in", "r_in", "h_in", "b_in"))
        ln_in = sem("ln_in")
        ln_used = sem("ln_used")
        dve_c, act_c, pool_c = sem("dve_c"), sem("act_c"), sem("pool_c")
        dt_mm, dt_a, dt_b, dt_c, dt_dve, acs_mm, dt_ready = (sem(n) for n in (
            "dt_mm", "dt_a", "dt_b", "dt_c", "dt_dve", "acs_mm", "dt_ready"))
        x_split = sem("x_split")
        w_high, w_low_p, w_low_v = sem("w_high"), sem("w_low_p"), sem("w_low_v")
        ch_mm, ch_seed, ch_conv, ch_silu = sem("ch_mm"), sem("ch_seed"), sem("ch_conv"), sem("ch_silu")
        cb_mm, cb_ready, btok_mm, btok_ready = sem("cb_mm"), sem("cb_ready"), sem("btok_mm"), sem("btok_ready")
        xt_mm, xt_ready = sem("xt_mm"), sem("xt_ready")
        dec_mm, dec_sub, dec_exp, dec_ready = sem("dec_mm"), sem("dec_sub"), sem("dec_exp"), sem("dec_ready")
        z_mm, z_ready, xw_ready, xd_ready = sem("z_mm"), sem("z_ready"), sem("xw_ready"), sem("xd_ready")
        st_mm, st_ready, yd_mm, yo_mm, y_gated, y_sq, y_ready = (sem(n) for n in (
            "st_mm", "st_ready", "yd_mm", "yo_mm", "y_gated", "y_sq", "y_ready"))
        yT_mm, yT_ready, yT_rest = sem("yT_mm"), sem("yT_ready"), sem("yT_rest")
        tb_mm, tb_row, tb_out, tb_in = sem("tb_mm"), sem("tb_row"), sem("tb_out"), sem("tb_in")
        var_ready, rstd_ready = sem("var_ready"), sem("rstd_ready")
        mix_mm = sem("mix_mm")
        h_ready = sem("h_ready")
        h_final = [sem(f"h_final{t}") for t in range(TB)]
        xn_ready = sem("xn_ready")
        hT_mm = sem("hT_mm")
        hT_a, hT_v = sem("hT_a"), sem("hT_v")
        aT_rest = sem("aT_rest")
        out_done = sem("out_done")
        att = {n: sem("att_" + n) for n in (
            "rev", "bias", "proj", "ev_a", "ev_v", "score", "logit", "negmax", "prob", "pt", "ptc", "pv", "oc",
            "ln", "lse", "wexp", "o", "oT", "oTa", "oTl")}
        moe = [{n: sem(f"moe{L}_" + n) for n in (
            "logit", "gsub", "gexp", "dsub", "dexp", "mask", "rank", "active", "place", "table", "turned",
            "turnedc", "item", "listed", "route", "sel", "gathered",
            "exT_a", "exT_v", "gate", "silu", "up", "hid", "tr", "hidT", "selgT", "down", "yex_a",
            "yex_v", "comb", "added", "end")} for L in range(2)]

        block = ctx.enter_context(nc.Block())

        def in_order(eng, s):
            n = [0]

            def link(ins):
                n[0] += 1
                ins.then_inc(s, 1)
                eng.wait_ge(s, n[0])
            return link

        def cols(w, c):
            return w[:, c:c + 512].rearrange("(k p) n -> p k n", p=P)

        def krows(w, r):
            return w[r:r + 512, :].rearrange("(k p) n -> p k n", p=P)

        def wide(j):
            return ring[:, j % RING, :].rearrange("p (k n) -> p k n", k=KD)

        def tall(j):
            return ring[:, j % RING, :].rearrange("p (k n) -> p k n", k=4)

        in_cols = [4096, 4608, 2048, 2560, 3072, 3584, 0, 512, 1024, 1536]
        pre = [(J_IN + i, wide, cols(in_w, c)) for i, c in enumerate(in_cols[:6])]
        pre += [(J_Z + 2 * i, wide, cols(in_w, c)) for i, c in enumerate(in_cols[6:])]
        pre += [(J_OUT + 2 * i, tall, krows(out_w, 512 * i)) for i in range(4)]
        mid = [(J_ATT + 2 * i, wide, cols(w, c)) for i, (w, c) in enumerate((
            (kv_w, 0), (q_w, 0), (kv_w, 1024), (kv_w, 1536), (kv_w, 512), (q_w, 512)))]
        mid += [(J_ATT + 12 + 2 * i, tall, krows(o_w, 512 * i)) for i in (0, 1)]

        def unit_buffer(u):
            kind, n = UNITS[u][:2]
            if kind == "V":
                return v[:, n % 2, (n // 2) * 512:(n // 2 + 1) * 512]
            return (kT if kind == "K" else qT)[:, n, :]

        def further_pairs(eng, L):
            return eng.value_load(small[0:1, L, NITEM:NITEM + 1], min_val=3, max_val=NITEM // 2 - 3)

        def split_low(eng, unit, i, done):
            eng.wait_ge(w_high, i)
            unit.tensor_tensor(w_split[:, i % NSPLIT, 1], wide(J_IN + i // 4)[:, :, (i % 4) * P:(i % 4 + 1) * P],
                               w_split[:, i % NSPLIT, 0], ALU.subtract).then_inc(done, 1)

        @block.sync
        def _(sp):
            sp.dma_start(hT[:, :, :], xT).then_inc(x_in, 16)
            sp.dma_start(wide(0)[:, :, 0:P], cols(in_w, in_cols[0])[:, :, 0:P]).then_inc(x_in, 16)

            def load(j, shape, src, pairs=None):
                if j >= RING:
                    n = j - RING + 1
                    sp.wait_ge(w_used, n if pairs is None else pairs * 6 + n)
                sp.dma_start(shape(j), src).then_inc(w_full[j % RING], 16)

            def load_pair(L, base, q, experts):
                for i, (w, shape) in enumerate(((gate_w, wide), (gate_w, wide), (up_w, wide), (up_w, wide),
                                                (down_w, tall), (down_w, tall))):
                    j = base + i
                    sp.wait_ge(w_used, q * 6 + (j - RING + 1))
                    src = w[L, bass.ds(experts[i % 2], 1)].rearrange("e (k p) n -> p (e k) n", p=P)
                    sp.dma_start(shape(j), src).then_inc(w_full[j % RING], 16)

            def load_moe(L, base, before):
                load_pair(L, base, before, (0, 1))
                sp.wait_ge(moe[L]["route"], 1)
                further = further_pairs(sp, L)
                with sp.Fori(0, further) as p:
                    e = [sp.value_load(small[0:1, L, bass.ds(p * 2 + 2 + i, 1)], min_val=0, max_val=E - 1)
                         for i in range(2)]
                    load_pair(L, base, p + (before + 1), e)
                return further + (before + 1)

            for j, shape, src in pre:
                if j:
                    load(j, shape, src)
                else:
                    sp.dma_start(wide(0)[:, :, P:512], cols(in_w, in_cols[0])[:, :, P:512]).then_inc(w_full[0], 16)
                    sp.dma_start(cst[:, :], consts).then_inc(c_in, 16)
            pairs0 = load_moe(0, J_MOE0, 0)
            for j, shape, src in mid:
                load(j, shape, src, pairs0)
            load_moe(1, J_MOE1, pairs0)
            for t in range(TB):
                sp.wait_ge(h_final[t], 1)
                sp.dma_start(out[0, t * P:(t + 1) * P, :], h[:, t, :]).then_inc(out_done, 16)
            sp.wait_ge(out_done, 16 * TB)

        def filled(eng, j, pairs=None):
            n = 16 * (j // RING + 1)
            eng.wait_ge(w_full[j % RING], n if pairs is None else pairs * 16 + n)

        CH = SLOT // 4

        def high_chunk(act, j, c, pairs=None):
            if c == 0:
                filled(act, j, pairs)
                n = j + 1 - RING + 1
                act.wait_ge(w_used, n if pairs is None else pairs * 6 + n)
            nc.scalar.activation(split_ring[:, (j + 1) % RING, c * CH:(c + 1) * CH],
                                 ring[:, j % RING, c * CH:(c + 1) * CH], ACT.Copy).then_inc(w_full[(j + 1) % RING], 4)

        def low_chunk(eng, unit, done, j, c, pairs=None):
            n = 16 * ((j + 1) // RING) + 4 * (c + 1)
            eng.wait_ge(w_full[(j + 1) % RING], n if pairs is None else pairs * 16 + n)
            here = slice(c * CH, (c + 1) * CH)
            unit.tensor_tensor(split_ring[:, j % RING, here], ring[:, j % RING, here],
                               split_ring[:, (j + 1) % RING, here], ALU.subtract).then_inc(done, 1)

        def high_low(j, k_tiles):
            return [split_ring[:, jj % RING, :].rearrange("p (k n) -> p k n", k=k_tiles) for jj in (j + 1, j)]

        def t_bank(n):
            return 0 if n == 0 else 4

        def token_transposes(pe, src, first_bank, done):
            for k in range(KD):
                for t in range(TB):
                    b = bank[first_bank + k // 2]
                    c = (k % 2) * S + t * P
                    last = nc.tensor.transpose(b[:, c:c + P], src[:, t, k * P:(k + 1) * P], ident)
                if k % 2:
                    last.then_inc(done, 1)

        @block.tensor
        def _(pe):
            mm = nc.tensor.matmul
            pe.wait_ge(x_in, 32)

            def channel_tile(i):
                j = J_IN + i // 4
                if i == 1 or i and i % 4 == 0:
                    filled(pe, j)
                if i >= 2:
                    pe.wait_ge(ch_conv, i - 1)
                if i == 0:
                    for k in range(KD):
                        last = mm(bank[0][:, 0:S], wide(j)[:, k, 0:P], hT[:, k, :], start=k == 0, stop=k == KD - 1)
                else:
                    if i == 1:
                        pe.wait_ge(x_split, 2)
                    if i % 3 == 1:
                        pe.wait_ge(w_low_v, (i + 2) // 3)
                    else:
                        pe.wait_ge(w_low_p, i - (i + 2) // 3)
                    high, low = w_split[:, i % NSPLIT, 0], w_split[:, i % NSPLIT, 1]
                    for n, (w, a) in enumerate(((high, xT_high), (high, xT_low), (low, xT_high))):
                        for k in range(KD):
                            last = mm(bank[i % 2][:, 0:S], w[:, k, :], a[:, k, :], start=n == 0 and k == 0,
                                      stop=n == 2 and k == KD - 1)
                last.then_inc(ch_mm, 1)
                if i % 4 == 3:
                    pe.drain().then_inc(w_used, 1)

            def xs_transpose(i):
                pe.wait_ge(ch_silu, 8 + i + 1)
                if i >= 2:
                    pe.wait_ge(xt_ready, i - 1)
                for t in range(TB):
                    last = nc.tensor.transpose(bank[4 + i % 2][:, t * P:(t + 1) * P],
                                               xcm[:, i % 2, t * P:(t + 1) * P], ident)
                last.then_inc(xt_mm, 1)

            for i in range(8):
                channel_tile(i)
                if i == 1:
                    pe.wait_ge(c_in, 16)
                    for t in range(TB):
                        for k in range(KD):
                            last = mm(bank[6][:, t * NH:(t + 1) * NH], hT[:, k, t * P:(t + 1) * P],
                                      cst[:, C_DTW + k * NH:C_DTW + (k + 1) * NH], start=k == 0, stop=k == KD - 1)
                    last.then_inc(dt_mm, 1)
                    pe.wait_ge(b_in, 16)
                    mm(bank[7][0:AH, 0:384], bp[:, 768:768 + AH], bp[:, 0:384], start=True,
                       stop=True).then_inc(tb_mm, 1)
            pe.wait_ge(dt_ready, 1)
            pe.wait_ge(tb_row, 1)
            for t in range(TB):
                mm(bank[7][:, t * NH:(t + 1) * NH], tri, dts[:, 2, t, :], start=True, stop=True)
            mm(bank[7][:, 64:64 + NH], ones, dts[:, 2, 0, :], start=True, stop=True).then_inc(acs_mm, 1)
            channel_tile(8)
            pe.wait_ge(ch_silu, 8)
            for c in range(TB):
                for g in range(G):
                    last = mm(bank[4 + c][:, g * P:(g + 1) * P], bcT[:, g, c * P:(c + 1) * P],
                              bcT[:, G + g, c * P:(c + 1) * P], start=True, stop=True)
            last.then_inc(cb_mm, 1)
            for g in range(G):
                last = nc.tensor.transpose(bank[6][:, g * P:(g + 1) * P], bcT[:, g, 0:P], ident)
            last.then_inc(btok_mm, 1)
            channel_tile(9)
            for i in range(10, 24):
                if i == 11:
                    pe.wait_ge(cb_ready, 1)
                    xs_transpose(0)
                if i > 10:
                    xs_transpose(i - 10)
                channel_tile(i)

            def y_transposes(g, first_bank):
                pe.wait_ge(y_ready, g + 1)
                for i in range(4 * g, 4 * g + 4):
                    for t in range(TB):
                        c = (i % 2) * S + t * P
                        last = nc.tensor.transpose(bank[first_bank + (i % 4) // 2][:, c:c + P],
                                                   y[:, g, t, (i % 4) * P:(i % 4 + 1) * P], ident)
                last.then_inc(yT_mm, 1)

            def z_tile(g, t):
                j = J_Z + 2 * g
                if g:
                    pe.wait_ge(z_ready, g)
                    pe.wait_ge(y_gated, g)
                w_high_, w_low_ = high_low(j, KD)
                for k in range(KD):
                    if k % 2 == 0:
                        pe.wait_ge(piece_low, 4 * g + k // 2 + 1)
                    for n, (a, w) in enumerate(((xT_high, w_high_), (xT_low, w_high_), (xT_high, w_low_))):
                        mm(bank[2 + t][:, :], a[:, k, t * P:(t + 1) * P], w[:, k, :], start=k == 0 and n == 0,
                           stop=k == KD - 1 and n == 2)

            z_tile(0, 0)
            xs_transpose(14)
            xs_transpose(15)
            pe.wait_ge(xt_ready, 16)
            pe.wait_ge(btok_ready, 1)
            for g in range(G):
                if g:
                    pe.wait_ge(st_ready, g)
                if g >= 2:
                    pe.wait_ge(yT_rest, 4 * (g - 1))
                for c in range(TB):
                    for r in range(HG):
                        b = bank[4 + 2 * c + r // 4]
                        a = dts[:, 2, c, g * HG + r:g * HG + r + 1]
                        last = mm(b[:, (r % 4) * P:(r % 4 + 1) * P], a.to_broadcast([P, P]), tri,
                                  start=True, stop=True)
                last.then_inc(dec_mm, 1)
                z_tile(g, 1)
                if g:
                    z_tile(g, 0)
                pe.drain().then_inc(z_mm, 1)
                pe.drain().then_inc(w_used, 2)
                pe.wait_ge(xw_ready, g + 1)
                pe.wait_ge(dec_sub, g + 1)
                mm(bank[4][:, :], btok[:, g, :], xw[:, :], start=True, stop=True).then_inc(st_mm, 1)
                if g:
                    y_transposes(g - 1, 6)
                pe.wait_ge(dec_ready, g + 1)
                for c in range(TB):
                    for r in range(HG):
                        last = mm(bank[c][:, r * HD:(r + 1) * HD], dec[:, c, r, :],
                                  xtok[:, g, c, r * HD:(r + 1) * HD], start=True, stop=True)
                last.then_inc(yd_mm, 1)
                pe.wait_ge(st_ready, g + 1)
                pe.wait_ge(z_ready, g + 1)
                mm(bank[3][:, :], bcT[:, G + g, P:2 * P], stT[:, :], start=True, stop=True).then_inc(yo_mm, 1)
            pe.wait_ge(yT_rest, 12)
            def out_block(i, tiles):
                if i < 12:
                    pe.wait_ge(piece_low, 16 + i + 1)
                else:
                    pe.wait_ge(w_low_v, 8 + (i - 12) + 1)
                w_high_, w_low_ = high_low(J_OUT + 2 * (i // 4), 4)
                for t in tiles:
                    for n, (a, w) in enumerate(((yT_high, w_high_), (yT_high, w_low_), (yT_low, w_high_))):
                        for c in range(2):
                            mm(bank[4 + 2 * t + c][:, :], a[:, i, t * P:(t + 1) * P],
                               w[:, i % 4, c * 512:(c + 1) * 512], start=i == 0 and n == 0,
                               stop=i == 15 and n == 2, skip_group_check=True)

            for i in range(12):
                if i == 8:
                    y_transposes(3, 0)
                out_block(i, range(TB))
                if i % 4 == 3:
                    pe.drain().then_inc(w_used, 2)
            pe.wait_ge(yT_rest, 16)
            for t in range(TB):
                for i in range(12, 16):
                    out_block(i, (t,))
                pe.drain().then_inc(mix_mm, 1)
            pe.drain().then_inc(w_used, 2)

            def keep_clock(n, b):
                for _ in range(n):
                    mm(bank[b][:, :], ident, cst[:, C_RW:C_RW + 512], start=True, stop=True)

            def normed(n, idle=(0, 0)):
                for t in range(TB):
                    keep_clock(idle[t], 4 - t_bank(n - 1))
                    pe.wait_ge(xn_ready, (n - 1) * TB + t + 1)
                    for k in range(KD):
                        c = (k % 2) * S + t * P
                        last = nc.tensor.transpose(bank[t_bank(n - 1) + k // 2][:, c:c + P], h[:, t, k * P:(k + 1) * P], ident)
                        if t == TB - 1 and k % 2:
                            last.then_inc(hT_mm, 1)
                if n != 2:
                    pe.wait_ge(hT_a, 2 * n)
                    pe.wait_ge(hT_v, 2 * n)

            def gather(m, wait):
                pe.wait_ge(m["sel"], wait)
                for k in range(KD):
                    for t in range(TB):
                        last = mm(bank[k // 4][:, (k % 4) * P:(k % 4 + 1) * P], h[:, t, k * P:(k + 1) * P],
                                  sel[:, t, :], start=t == 0, stop=t == TB - 1)
                last.then_inc(m["gathered"], 1)

            def gate_up(L, base, q, before):
                m = moe[L]
                pe.wait_ge(m["exT_a"], q + 1)
                pe.wait_ge(m["exT_v"], q + 1)
                for first, out_bank, name in ((0, 2, "gate"), (2, 3, "up")):
                    for k in range(KD):
                        for e in range(2):
                            if k == 0:
                                filled(pe, base + first + e, q if before is None else before + q)
                            last = mm(bank[out_bank][64 * e:64 * e + 64, :], exT[:, k, 64 * e:64 * e + 64],
                                      wide(base + first + e)[:, k, :], start=k == 0, stop=k == KD - 1)
                            if k == KD - 1 and e == 0:
                                last.then_inc(w_used, 1)
                    last.then_inc(m[name], 1)
                    pe.drain().then_inc(w_used, 1)

            def down_combine(L, base, q, before, following):
                m = moe[L]
                if following:
                    gather(m, q + 2)
                pe.wait_ge(m["hid"], q + 2)
                pe.wait_ge(m["added"], q * 4 + 1)
                for k in range(4):
                    nc.tensor.transpose(bank[4][:, k * P:(k + 1) * P], hid[:, k * P:(k + 1) * P], ident)
                for t in range(TB):
                    last = nc.tensor.transpose(bank[7][:, t * P:(t + 1) * P], selg[:, t, :], ident)
                last.then_inc(m["tr"], 1)
                pe.wait_ge(m["hidT"], q + 1)
                for k in range(4):
                    for c in range(2):
                        for e in range(2):
                            if k == 0 and c == 0:
                                filled(pe, base + 4 + e, q if before is None else before + q)
                            last = mm(bank[5 + c][64 * e:64 * e + 64, :], hidT[:, k, 64 * e:64 * e + 64],
                                      tall(base + 4 + e)[:, k, c * 512:(c + 1) * 512], start=k == 0, stop=k == 3,
                                      skip_group_check=True)
                            if k == 3 and c == 1 and e == 0:
                                last.then_inc(w_used, 1)
                last.then_inc(m["down"], 1)
                pe.drain().then_inc(w_used, 1)
                pe.wait_ge(m["selgT"], q + 1)
                for i, (t, c) in enumerate(((0, 0), (0, 1), (1, 0), (1, 1))):
                    if i == 0:
                        pe.wait_ge(m["yex_a"], q + 1)
                    if i == 1:
                        pe.wait_ge(m["yex_v"], q + 1)
                    if i >= 2:
                        pe.wait_ge(m["added"], q * 4 + i)
                    mm(bank[7 if i % 2 == 0 else 4][:, :], selgT[:, t * P:(t + 1) * P],
                       yex[:, c * 512:(c + 1) * 512], start=True, stop=True).then_inc(m["comb"], 1)

            def experts(L, base, before):
                m = moe[L]
                for t in range(TB):
                    for k in range(KD):
                        c = C_RW + (L * KD + k) * 36
                        last = mm(bank[0][:, t * 36:(t + 1) * 36], hT[:, k, t * P:(t + 1) * P], cst[:, c:c + 36],
                                  start=k == 0, stop=k == KD - 1)
                last.then_inc(m["logit"], 1)
                keep_clock(3, 6)
                pe.wait_ge(m["mask"], 1)
                mask = rt[:, 0:TB * E].rearrange("p (t e) -> p t e", t=TB)
                b = bank[4]
                mm(b[:, 0:E], stri, mask[:, 0, :], start=True, stop=True)
                mm(b[:, E:2 * E], stri, mask[:, 1, :], start=True, stop=False)
                mm(b[:, E:2 * E], ones, mask[:, 0, :], start=False, stop=True)
                for i in range(NBLK):
                    for t in range(TB):
                        last = mm(b[i * E:(i + 1) * E, 2 * E:2 * E + 1], mask[:, t, :], ones[:, 0:1],
                                  start=t == 0, stop=t == TB - 1)
                last.then_inc(m["rank"], 1)
                pe.wait_ge(h_ready, L * 2 + 1)
                gather(m, 1)
                pe.wait_ge(m["active"], 1)
                active = rt[:, 380:381]
                mm(bank[5][:, 0:1], stri, active, start=True, stop=True).then_inc(m["place"], 1)
                pe.wait_ge(m["table"], 1)
                for a in range(2):
                    for t in range(TB):
                        c = (a * TB + t) * P
                        last = nc.tensor.transpose(bank[6][:, c:c + P], tables[:, a, t, :], ident)
                last.then_inc(m["turned"], 1)
                pe.wait_ge(m["item"], 1)
                mm(bank[5][0:1, 64:64 + NITEM], cst[:, C_EXP:C_EXP + 1], is_item, start=True, stop=True)
                mm(bank[5][0:1, 128:128 + NITEM], ones[:, 0:1], is_item, start=True, stop=True)
                pe.wait_ge(m["turnedc"], 1)
                for i in range(2 * TB):
                    last = mm(bank[7][:, i * NITEM:(i + 1) * NITEM], tablesT[:, i * P:(i + 1) * P], is_item,
                              start=True, stop=True)
                last.then_inc(m["listed"], 1)
                gate_up(L, base, 0, before)
                pe.wait_ge(m["route"], 1)
                further = further_pairs(pe, L)
                with pe.Fori(0, further) as q:
                    down_combine(L, base, q, before, True)
                    gate_up(L, base, q + 1, before)
                down_combine(L, base, further, before, False)
                return further + 1

            normed(1, (0, 3))
            pairs0 = experts(0, J_MOE0, None)
            pe.wait_ge(tb_in, 16)
            for i in range(8):
                if i >= 2:
                    pe.wait_ge(att["bias"], i - 1)
                mm(bank[i % 2][:, :], cst[:, C_REV:C_REV + P], bias[:, 2 * i:2 * i + 2, :], start=True,
                   stop=True).then_inc(att["rev"], 1)
            normed(2)

            def project(u):
                kind, n, j, first, last_use = UNITS[u]
                if u == 0:
                    pe.wait_ge(att["bias"], 8)
                if u >= 2:
                    pe.wait_ge(att["ev_a"] if u % 2 == 0 else att["ev_v"], (u - 2) // 2 + 1)
                w_high_, w_low_ = high_low(j, KD)
                for n3, (w, a) in enumerate(((w_high_, aT_high), (w_low_, aT_high), (w_high_, aT_low))):
                    if u == 0 and n3 == 2:
                        pe.wait_ge(aT_rest, 4)
                    for k in range(KD):
                        if first and n3 == 0 and k % 2 == 0:
                            pe.wait_ge(piece_low, 28 + 2 * (j - J_ATT) + k // 2 + 1)
                        if u == 0 and n3 == 0 and k % 2 == 0:
                            pe.wait_ge(hT_v if k // 2 % 2 else hT_a, 2 + k // 4 + 1)
                        ends = dict(start=n3 == 0 and k == 0, stop=n3 == 2 and k == KD - 1)
                        if kind == "V":
                            last = mm(bank[u % 2][:, :], a[:, k, (n % 2) * P:(n % 2 + 1) * P], w[:, k, :], **ends)
                        else:
                            last = mm(bank[u % 2][:, 0:S], w[:, k, (n % 4) * P:(n % 4 + 1) * P], a[:, k, :], **ends)
                last.then_inc(att["proj"], 1)
                if last_use:
                    pe.drain().then_inc(w_used, 2)

            def projected(u):
                pe.wait_ge(att["ev_a"], u // 2 + 1)
                pe.wait_ge(att["ev_v"], (u + 1) // 2)

            def scores(n):
                projected(UNIT_OF_HEADS[n // 2])
                if n >= 2:
                    pe.wait_ge(att["prob"], n - 1)
                b, r, k = bank[4 + n % 2], HD * (n % 2), n // 2
                mm(b[:, 0:P], qT[r:r + HD, k, 0:P], kT[r:r + HD, k, 0:P], start=True, stop=True)
                mm(b[:, P:P + S], qT[r:r + HD, k, P:S], kT[r:r + HD, k, :], start=True,
                   stop=True).then_inc(att["score"], 1)

            def turn(n):
                pe.wait_ge(att["prob"], n + 1)
                if n >= 2:
                    pe.wait_ge(att["ptc"], n - 1)
                for i in range(3):
                    last = nc.tensor.transpose(bank[6 + n % 2][:, i * P:(i + 1) * P],
                                               scb[:, n % 2, i * P:(i + 1) * P], ident)
                last.then_inc(att["pt"], 1)

            def values(n):
                projected(UNIT_OF_V[n // 8])
                pe.wait_ge(att["ptc"], n + 1)
                if n % 4 == 0 and n >= 8:
                    pe.wait_ge(att["oc"], n // 4 - 1)
                b, c, n2 = bank[2 + n // 4 % 2], (n % 4) * P, n * HD
                mm(b[:, c:c + HD], pT[:, n % 2, 0:P], v[:, 0, n2:n2 + HD], start=True, stop=True)
                mm(b[:, c + HD:c + P], pT[:, n % 2, P:2 * P], v[:, 0, n2:n2 + HD], start=True, stop=False)
                mm(b[:, c + HD:c + P], pT[:, n % 2, 2 * P:3 * P], v[:, 1, n2:n2 + HD], start=False,
                   stop=True).then_inc(att["pv"], 1)

            for kind, n in ATT_ORDER:
                if kind == "project":
                    project(n)
                elif kind == "scores":
                    scores(n)
                elif kind == "turn":
                    turn(n)
                else:
                    values(n)
            keep_clock(5, 4)
            pe.wait_ge(att["o"], TB)
            token_transposes(pe, osb, 4, att["oT"])
            def o_block(k, tiles):
                if k < 4:
                    pe.wait_ge(piece_low, 28 + 24 + k + 1)
                else:
                    pe.wait_ge(w_low_v, 12 + (k - 4) + 1)
                pe.wait_ge(att["oTl"], k // 2 + 1)
                w_high_, w_low_ = high_low(J_ATT + 12 + 2 * (k // 4), 4)
                for t in tiles:
                    for n, (a, w) in enumerate(((oT_high, w_high_), (oT_high, w_low_), (oT_low, w_high_))):
                        for c in range(2):
                            mm(bank[2 * t + c][:, :], a[:, k, t * P:(t + 1) * P],
                               w[:, k % 4, c * 512:(c + 1) * 512], start=k == 0 and n == 0,
                               stop=k == KD - 1 and n == 2, skip_group_check=True)

            for k in range(4):
                o_block(k, range(TB))
            pe.drain().then_inc(w_used, 2)
            for t in range(TB):
                for k in range(4, KD):
                    o_block(k, (t,))
                pe.drain().then_inc(mix_mm, 1)
            pe.drain().then_inc(w_used, 2)
            normed(3, (0, 3))
            experts(1, J_MOE1, pairs0)

        @block.gpsimd
        def _(pool):
            T = nc.gpsimd.tensor_tensor
            pool.memset(minus_half, -0.5).then_inc(pool_c, 1)
            pool.wait_ge(pool_c, 1)
            for i in range(1, 24):
                if i % 3 != 1:
                    split_low(pool, nc.gpsimd, i, w_low_p)
                if i >= 20:
                    low_chunk(pool, nc.gpsimd, piece_low, J_Z, i - 20)
                if i == 10:
                    pool.wait_ge(tb_row, 1)
                    pool.dma_start(toeplitz_rows, trow[:, :]).then_inc(tb_out, 16)
            for g in range(G):
                heads = slice(g * HG, (g + 1) * HG)
                if g == 0:
                    pool.wait_ge(r_in, 16)
                pool.wait_ge(xt_ready, 4 * g + 4)
                pool.wait_ge(dt_c, 1)
                if g:
                    pool.wait_ge(st_mm, g)
                T(xw.rearrange("p (r c) -> p r c", r=HG), xtok[:, g, 0, :].rearrange("p (r c) -> p r c", r=HG),
                  dts[:, 7, 0, heads].unsqueeze(2).to_broadcast([P, HG, HD]), ALU.mult).then_inc(xw_ready, 1)
                if g:
                    pool.wait_ge(y_gated, g)
                for t in range(TB):
                    T(xd[:, t, :].rearrange("p (r c) -> p r c", r=HG),
                      xtok[:, g, t, :].rearrange("p (r c) -> p r c", r=HG),
                      row[:, R_DS + g * HG:R_DS + (g + 1) * HG].unsqueeze(2).to_broadcast([P, HG, HD]),
                      ALU.mult).then_inc(xd_ready, 1)
                for c in range(4):
                    low_chunk(pool, nc.gpsimd, piece_low, J_Z + 2 * (g + 1), c)
                st = stats[:, g * TB:(g + 1) * TB]
                pool.wait_ge(var_ready, g + 1)
                T(st, st, minus_half, ALU.pow).then_inc(rstd_ready, 1)
            for i in (1, 2):
                for c in range(4):
                    low_chunk(pool, nc.gpsimd, piece_low, J_OUT + 2 * i, c)
            pairs0 = [None]

            def low_chunks(first, end):
                for i in range(first, end):
                    for c in range(4):
                        low_chunk(pool, nc.gpsimd, piece_low, J_ATT + 2 * i, c, pairs0[0])

            for n, st in enumerate((lnst, lnst, lnst2, lnst)):
                if n == 1:
                    pool.wait_ge(moe[0]["route"], 1)
                    pairs0[0] = further_pairs(pool, 0) + 1
                    low_chunks(0, 1)
                for t in range(TB):
                    pool.wait_ge(var_ready, G + TB * n + t + 1)
                    rs = st[:, 28 + t:29 + t]
                    T(rs, rs, minus_half[:, 0:1], ALU.pow).then_inc(rstd_ready, 1)
                if n == 0:
                    pool.wait_ge(tb_out, 16)
                    pool.wait_ge(mix_mm, TB)
                    skewed = bass.AP(tensor=toeplitz_rows.tensor, offset=toeplitz_rows.offset,
                                     ap=[[1, P], [384, AH], [1, S]])
                    pool.dma_start(bias[:, :, :], skewed).then_inc(tb_in, 16)
                if n == 1:
                    low_chunks(1, 7)
                pool.wait_ge(ln_in, 32 * (n + 1))
                if n < 3:
                    pool.wait_ge(hT_mm, 4 * (n + 1))
                else:
                    pool.wait_ge(xn_ready, TB * 3 + 2)
                for t in range(TB):
                    if n < 3 or t == 1:
                        T(h[:, t, :], h[:, t, :], lnw[:, 0, :], ALU.mult).then_inc(pool_c, 1)
                        pool.wait_ge(pool_c, 2 + TB * n + (t if n < 3 else 0))
                        last = T(h[:, t, :], h[:, t, :], lnw[:, 1, :], ALU.add)
                last.then_inc(h_ready if n < 3 else h_final[1], 1)

        @block.scalar
        def _(act):
            A = nc.scalar.activation
            link = in_order(act, act_c)
            act.dma_start(row[:, :], rows.partition_broadcast(P)).then_inc(r_in, 16)
            act.dma_start(bp[:, :], bias_pack).then_inc(b_in, 16)
            def load_ln(n):
                if n:
                    act.wait_ge(h_ready, n)
                for a, w in ((0, ln_g), (1, ln_b)):
                    act.dma_start(lnw[:, a, :], w[n // 2, n % 2].partition_broadcast(P)).then_inc(ln_in, 16)

            act.wait_ge(x_in, 32)
            A(xT_high, hT[:, :, :], ACT.Copy).then_inc(x_split, 1)

            def split_high(i):
                if i < 24:
                    if i % 4 == 0 or i == 1:
                        filled(act, J_IN + i // 4)
                    if i > NSPLIT:
                        act.wait_ge(ch_mm, i - NSPLIT + 1)
                    A(w_split[:, i % NSPLIT, 0], wide(J_IN + i // 4)[:, :, (i % 4) * P:(i % 4 + 1) * P],
                      ACT.Copy).then_inc(w_high, 1)

            for i in range(1, NSPLIT):
                split_high(i)
            act.wait_ge(c_in, 16)
            cw = lambda i, k: cst[:, C_CW + i * 4 + k:C_CW + i * 4 + k + 1]
            chan = [16 + i if i < 8 else i - 8 for i in range(24)]

            def seed(i):
                act.wait_ge(ch_mm, i + 1)
                if i >= 2:
                    act.wait_ge(ch_silu, i - 1)
                A(conv_acc[:, i % 2, :], bank[i % 2][:, 0:S], ACT.Identity, scale=cw(chan[i], 3),
                  bias=cst[:, C_CB + chan[i]:C_CB + chan[i] + 1]).then_inc(ch_seed, 1)

            def silu(i):
                act.wait_ge(ch_conv, i + 1)
                if i >= 10:
                    act.wait_ge(xt_mm, i - 9)
                dst = bcT[:, i, :] if i < 8 else xcm[:, i % 2, :]
                A(dst, conv_acc[:, i % 2, :], ACT.Silu).then_inc(ch_silu, 1)

            def xt_copy(i):
                act.wait_ge(xt_mm, i + 1)
                A(xtok[:, i // 4, :, i % 4 * P:(i % 4 + 1) * P], bank[4 + i % 2][:, 0:S].rearrange("p (t c) -> p t c", t=TB),
                  ACT.Copy).then_inc(xt_ready, 1)

            def dt_steps():
                act.wait_ge(dt_a, 1)
                A(dts[:, 1, :, :], dts[:, 1, :, :], ACT.Exp).then_inc(dt_b, 1)
                act.wait_ge(r_in, 16)
                A(dts[:, 9, 0, :], row[:, R_AL:R_AL + NH], ACT.Exp).then_inc(dt_b, 1)
                act.wait_ge(dt_b, 2)
                A(dts[:, 1, :, :], dts[:, 1, :, :], ACT.Ln, bias=1.0).then_inc(dt_b, 1)

            for i in range(24):
                if i:
                    silu(i - 1)
                if i >= 11:
                    xt_copy(i - 11)
                seed(i)
                split_high(i + NSPLIT)
                if 17 <= i < 21:
                    high_chunk(act, J_Z, i - 17)
                if i == 3:
                    dt_steps()
                if i == 10:
                    act.wait_ge(btok_mm, 1)
                    A(btok.rearrange("p g n -> p (g n)"), bank[6][:, :], ACT.Copy).then_inc(btok_ready, 1)
            silu(23)
            for i in range(13, 16):
                xt_copy(i)
            act.wait_ge(dt_dve, 1)
            A(dts[:, 5, :, :], dts[:, 3, :, :], ACT.Exp).then_inc(dt_b, 1)
            A(dts[:, 6, :, :], dts[:, 4, :, :], ACT.Exp).then_inc(dt_b, 1)
            def yT_copy(g, first_bank):
                act.wait_ge(yT_mm, g + 1)
                for i in range(4 * g, 4 * g + 4):
                    A(yT_high[:, i, :], bank[first_bank + (i % 4) // 2][:, (i % 2) * S:(i % 2 + 1) * S], ACT.Copy,
                      scale=cst[:, C_NW + i:C_NW + i + 1]).then_inc(yT_ready, 1)

            for g in range(G):
                act.wait_ge(dec_sub, g + 1)
                for c in range(TB):
                    A(dec[:, c, :, :], dec[:, c, :, :], ACT.Exp).then_inc(dec_exp, 1)
                for c in range(4):
                    high_chunk(act, J_Z + 2 * (g + 1), c)
                act.wait_ge(z_mm, g + 1)
                if g == G - 1:
                    act.dma_start(h[:, :, :], x[0].rearrange("(t p) d -> p t d", p=P)).then_inc(h_in, 16)
                    load_ln(0)
                if g >= 2:
                    act.wait_ge(y_gated, g - 1)
                for t in range(TB):
                    last = A(zs[:, g % 2, t, :], bank[2 + t][:, :], ACT.Silu)
                last.then_inc(z_ready, 1)
                act.wait_ge(st_mm, g + 1)
                if g:
                    act.wait_ge(yo_mm, g)
                A(stT[:, :], bank[4][:, :], ACT.Copy).then_inc(st_ready, 1)
                if g:
                    yT_copy(g - 1, 6)
                act.wait_ge(y_gated, g + 1)
                for t in range(TB):
                    if t or g:
                        act.wait_ge(y_sq, g * TB + t)
                    A(sq[:, :], y[:, g, t, :], ACT.Square,
                      accum_out=stats[:, g * TB + t:g * TB + t + 1]).then_inc(y_sq, 1)
            for i in range(1, 4):
                for c in range(4):
                    high_chunk(act, J_OUT + 2 * i, c)
            yT_copy(3, 0)

            def copy_hT(n):
                for i in (0, 2):
                    act.wait_ge(hT_mm, 4 * n + i + 1)
                    for k in (2 * i, 2 * i + 1):
                        g, b = C_LNG + n * KD + k, C_LNB + n * KD + k
                        last = A(hT[:, k, :], bank[t_bank(n) + i][:, (k % 2) * S:(k % 2 + 1) * S], ACT.Identity,
                                 scale=cst[:, g:g + 1], bias=cst[:, b:b + 1])
                        if n == 1:
                            last = A(aT_high[:, k, :], bank[4 + i][:, (k % 2) * S:(k % 2 + 1) * S], ACT.Identity,
                                     scale=cst[:, g:g + 1], bias=cst[:, b:b + 1])
                    last.then_inc(hT_a, 1)

            def copy_exT(m, n):
                act.wait_ge(m["gathered"], n)
                A(exT[:, 0:4, :], bank[0][:, :].rearrange("p (k c) -> p k c", k=4),
                  ACT.Copy).then_inc(m["exT_a"], 1)

            def expert_pair(m, q, following):
                act.wait_ge(m["gate"], q + 1)
                act.wait_ge(m["hid"], q + 1)
                A(silu_g[:, :], bank[2][:, :], ACT.Silu).then_inc(m["silu"], 1)
                if following:
                    copy_exT(m, q + 2)
                act.wait_ge(m["tr"], q + 1)
                act.wait_ge(m["added"], q * 4 + 1)
                A(selgT[:, :], bank[7][:, 0:S], ACT.Copy).then_inc(m["selgT"], 1)
                act.wait_ge(m["down"], q + 1)
                A(yex[:, 0:512], bank[5][:, :], ACT.Copy).then_inc(m["yex_a"], 1)

            def experts(L):
                m = moe[L]
                act.wait_ge(m["gsub"], 1)
                ge = rt[:, 64:72]
                A(ge, ge, ACT.Exp).then_inc(m["gexp"], 1)
                act.wait_ge(m["dsub"], 1)
                A(rt[:, 72:74], rt[:, 72:74], ACT.Exp).then_inc(m["dexp"], 1)
                copy_exT(m, 1)
                act.wait_ge(m["turned"], 1)
                A(tablesT, bank[6][:, :], ACT.Copy).then_inc(m["turnedc"], 1)
                act.wait_ge(h_ready, L * 2 + 1)
                A(yacc[:, :, :], h[:, :, :], ACT.Copy, scale=ALPHA).then_inc(m["added"], 1)
                act.wait_ge(m["route"], 1)
                further = further_pairs(act, L)
                with act.Fori(0, further) as q:
                    expert_pair(m, q, True)
                expert_pair(m, further, False)
                return further + 1

            copy_hT(0)
            load_ln(1)
            pairs0 = experts(0)
            chunks = iter([(J_ATT + 2 * i, c) for i in range(8) for c in range(4)])

            def high_chunks(n):
                for _ in range(n):
                    high_chunk(act, *next(chunks), pairs0)

            high_chunks(4)
            for i in range(8):
                act.wait_ge(att["rev"], i + 1)
                A(bias[:, 2 * i:2 * i + 2, :], bank[i % 2][:, :].rearrange("p (h c) -> p h c", h=2),
                  ACT.Copy).then_inc(att["bias"], 1)
            copy_hT(1)
            high_chunks(4)

            def projected(u):
                act.wait_ge(att["proj"], u + 1)
                A(unit_buffer(u), bank[u % 2][:, 0:512 if UNITS[u][0] == "V" else S],
                  ACT.Copy).then_inc(att["ev_a"], 1)

            def probabilities(n):
                act.wait_ge(att["negmax"], n + 1)
                A(scb[:, n % 2, 0:P], scb[:, n % 2, 0:P], ACT.Exp, bias=am[:, 1, 0, n:n + 1],
                  accum_out=am[:, 2, 0, n:n + 1])
                A(scb[:, n % 2, P:384], scb[:, n % 2, P:384], ACT.Exp, bias=am[:, 1, 1, n:n + 1],
                  accum_out=am[:, 2, 1, n:n + 1]).then_inc(att["prob"], 1)

            def pt_copy(n):
                act.wait_ge(att["pt"], n + 1)
                if n >= 2:
                    act.wait_ge(att["pv"], n - 1)
                A(pT[:, n % 2, :], bank[6 + n % 2][:, 0:384], ACT.Copy).then_inc(att["ptc"], 1)

            def o_copy(n):
                act.wait_ge(att["pv"], n + 1)
                A(osb[:, :, (n - 3) * HD:(n + 1) * HD].rearrange("p t (j c) -> p j t c", j=4),
                  bank[2 + n // 4 % 2][:, :].rearrange("p (j t c) -> p j t c", j=4, t=TB),
                  ACT.Copy).then_inc(att["oc"], 1)

            for kind, n in ATT_ORDER:
                if kind == "project":
                    if n % 2 == 0:
                        projected(n)
                    high_chunks(CHUNKS_AFTER.get(n, 0))
                elif kind == "scores":
                    probabilities(n)
                    if n == AH - 1:
                        act.wait_ge(att["prob"], AH)
                        A(am[:, 3, :, :], am[:, 2, :, :], ACT.Ln).then_inc(att["ln"], 1)
                elif kind == "turn":
                    pt_copy(n)
                elif kind == "values" and n % 4 == 3:
                    if n == AH - 1:
                        act.wait_ge(att["lse"], 1)
                        A(am[:, 6, :, 0:3], am[:, 6, :, 0:3], ACT.Exp).then_inc(att["wexp"], 1)
                    o_copy(n)
            load_ln(2)
            high_chunks(4)
            for i in (0, 2):
                act.wait_ge(att["oT"], i + 1)
                A(oT_high[:, 2 * i:2 * i + 2, :], bank[4 + i][:, :].rearrange("p (k s) -> p k s", k=2),
                  ACT.Copy).then_inc(att["oTa"], 1)
            copy_hT(2)
            load_ln(3)
            experts(1)

        @block.vector
        def _(dve):
            V = nc.vector
            link = in_order(dve, dve_c)
            cw = lambda i, k: cst[:, C_CW + i * 4 + k:C_CW + i * 4 + k + 1]
            chan = [16 + i if i < 8 else i - 8 for i in range(24)]
            def dt_steps():
                dve.wait_ge(dt_mm, 1)
                dve.wait_ge(r_in, 16)
                link(V.tensor_tensor(dts[:, 0, :, :], bank[6][:, 0:64].rearrange("p (t h) -> p t h", t=TB),
                                     row[:, R_DTB:R_DTB + NH].unsqueeze(1).to_broadcast([P, TB, NH]), ALU.add))
                link(V.tensor_scalar(dts[:, 2, :, :], dts[:, 0, :, :], -1.0, None, ALU.mult))
                V.tensor_tensor(dts[:, 1, :, :], dts[:, 0, :, :], dts[:, 2, :, :], ALU.min).then_inc(dt_a, 1)
                link(V.tensor_scalar(dts[:, 8, :, :], dts[:, 0, :, :], 0.0, None, ALU.max))

            def dt_end():
                dve.wait_ge(dt_b, 3)
                link(V.tensor_tensor(dts[:, 8, :, :], dts[:, 8, :, :], dts[:, 1, :, :], ALU.add))
                V.scalar_tensor_tensor(dts[:, 2, :, :], dts[:, 8, :, :], -1.0,
                                       dts[:, 9, 0:1, :].to_broadcast([P, TB, NH]), ALU.mult,
                                       ALU.mult).then_inc(dt_ready, 1)
                dve.wait_ge(tb_mm, 1)
                V.tensor_tensor(trow[:, :], bank[7][0:AH, 0:384], bp[0:AH, 384:768], ALU.add).then_inc(tb_row, 1)

            dve.wait_ge(x_split, 1)
            V.tensor_tensor(xT_low, hT[:, :, :], xT_high, ALU.subtract).then_inc(x_split, 1)
            split_low(dve, V, 1, w_low_v)
            for i in range(24):
                if i == 3:
                    dt_steps()
                if i == 5:
                    dt_end()
                if i == 9:
                    dve.wait_ge(cb_mm, 1)
                    for c in range(TB):
                        ins = V.tensor_tensor(cbm[:, c, :, :], bank[4 + c][:, :].rearrange("p (g i) -> p g i", g=G),
                                              tri.unsqueeze(1).to_broadcast([P, G, P]), ALU.mult)
                    ins.then_inc(cb_ready, 1)
                dve.wait_ge(ch_seed, i + 1)
                for s in (1, 2, 3):
                    ins = V.scalar_tensor_tensor(conv_acc[:, i % 2, s:S], bank[i % 2][:, 0:S - s],
                                                 cw(chan[i], 3 - s), conv_acc[:, i % 2, s:S], ALU.mult, ALU.add)
                    if s < 3:
                        link(ins)
                    else:
                        ins.then_inc(ch_conv, 1)
                if i % 3 == 1 and i + 3 < 24:
                    split_low(dve, V, i + 3, w_low_v)
                if i == 8:
                    dve.wait_ge(acs_mm, 1)
                    acs_ps = bank[7][:, 0:64].rearrange("p (t h) -> p t h", t=TB)
                    link(V.tensor_copy(dts[:, 3, :, :], acs_ps))
                    V.tensor_tensor(dts[:, 4, 0, :], bank[7][:, 64:96], dts[:, 3, 0, :], ALU.subtract)
                    V.tensor_copy(dts[:, 4, 1, :], dts[:, 3, 1, :]).then_inc(dt_dve, 1)
            dve.wait_ge(dt_b, 5)
            V.tensor_tensor(dts[:, 7, 0, :], dts[:, 6, 0, :], dts[:, 8, 0, :], ALU.mult).then_inc(dt_c, 1)
            dve.wait_ge(tb_out, 16)

            def yT_split(g, first_bank):
                for i in range(4 * g, 4 * g + 4):
                    if i % 2 == 0:
                        dve.wait_ge(yT_ready, i + 2)
                    V.scalar_tensor_tensor(yT_low[:, i, :], bank[first_bank + (i % 4) // 2][:, (i % 2) * S:(i % 2 + 1) * S],
                                           cst[:, C_NW + i:C_NW + i + 1], yT_high[:, i, :], ALU.mult,
                                           ALU.subtract).then_inc(yT_rest, 1)

            for g in range(G):
                dve.wait_ge(dec_mm, g + 1)
                if g:
                    dve.wait_ge(yd_mm, g)
                for c in range(TB):
                    for r in range(HG):
                        hh = g * HG + r
                        ins = V.tensor_scalar(dec[:, c, r, :], bank[4 + 2 * c + r // 4][:, (r % 4) * P:(r % 4 + 1) * P],
                                              dts[:, 3, c, hh:hh + 1], 0.0, ALU.subtract, ALU.min)
                ins.then_inc(dec_sub, 1)
                for c in range(TB):
                    dve.wait_ge(dec_exp, g * TB + c + 1)
                    for r in range(HG):
                        hh = g * HG + r
                        ins = V.scalar_tensor_tensor(dec[:, c, r, :], dec[:, c, r, :], dts[:, 8, c, hh:hh + 1],
                                                     cbm[:, c, g, :], ALU.mult, ALU.mult)
                ins.then_inc(dec_ready, 1)
                if g:
                    yT_split(g - 1, 6)
                dve.wait_ge(yd_mm, g + 1)
                dve.wait_ge(xd_ready, TB * (g + 1))
                for t in range(TB):
                    link(V.tensor_tensor(y[:, g, t, :], bank[t][:, :], xd[:, t, :], ALU.add))
                dve.wait_ge(yo_mm, g + 1)
                ea = dts[:, 5, 1, g * HG:(g + 1) * HG].unsqueeze(2).to_broadcast([P, HG, HD])
                link(V.tensor_tensor(xd[:, 1, :].rearrange("p (r c) -> p r c", r=HG),
                                     bank[3][:, :].rearrange("p (r c) -> p r c", r=HG), ea, ALU.mult))
                link(V.tensor_tensor(y[:, g, 1, :], y[:, g, 1, :], xd[:, 1, :], ALU.add))
                dve.wait_ge(z_ready, g + 1)
                V.tensor_tensor(y[:, g, :, :], y[:, g, :, :], zs[:, g % 2, :, :], ALU.mult).then_inc(y_gated, 1)
                dve.wait_ge(y_sq, TB * (g + 1))
                st = stats[:, g * TB:(g + 1) * TB]
                V.tensor_scalar(st, st, 1.0 / 512, EPS, ALU.mult, ALU.add).then_inc(var_ready, 1)
                dve.wait_ge(rstd_ready, g + 1)
                for t in range(TB):
                    ins = V.tensor_scalar(y[:, g, t, :], y[:, g, t, :], st[:, t:t + 1], None, ALU.mult)
                ins.then_inc(y_ready, 1)
            yT_split(3, 0)
            for c in range(4):
                low_chunk(dve, V, w_low_v, J_OUT + 6, c)

            def layer_norm(n, src, mix, st):
                if n:
                    dve.wait_ge(h_ready, n)
                sums = st[:, 0:24].rearrange("p (t c s) -> p t c s", t=TB, c=2)
                mv = st[:, 24:28].rearrange("p (t s) -> p t s", t=TB)
                rs = st[:, 28:30]

                def normalise(t):
                    dve.wait_ge(rstd_ready, G + TB * n + t + 1)
                    V.tensor_scalar(h[:, t, :], src[:, t, :], mv[:, t, 0:1], rs[:, t:t + 1],
                                    ALU.subtract, ALU.mult).then_inc(xn_ready, 1)

                for t in range(TB):
                    if mix:
                        dve.wait_ge(mix_mm, n // 2 * TB + t + 1)
                    for c in range(2):
                        cc = slice(c * 512, (c + 1) * 512)
                        if mix:
                            link(V.scalar_tensor_tensor(h[:, t, cc], h[:, t, cc], ALPHA, mix(t, c), ALU.mult, ALU.add))
                        link(V.bn_stats(sums[:, t, c, :], src[:, t, cc]))
                    link(V.bn_aggr(mv[:, t, :], sums[:, t, :, :].rearrange("p c s -> p (c s)")))
                    V.tensor_scalar(rs[:, t:t + 1], mv[:, t, 1:2], EPS, None, ALU.add).then_inc(var_ready, 1)
                    if mix:
                        normalise(t)
                if not mix:
                    for t in range(TB):
                        normalise(t)
                if n == 3:
                    dve.wait_ge(xn_ready, TB * 3 + 1)
                    dve.wait_ge(ln_in, 32 * 4)
                    link(V.tensor_tensor(h[:, 0, :], h[:, 0, :], lnw[:, 0, :], ALU.mult))
                    V.tensor_tensor(h[:, 0, :], h[:, 0, :], lnw[:, 1, :], ALU.add).then_inc(h_final[0], 1)

            def copy_hT(n):
                for i in (1, 3):
                    dve.wait_ge(hT_mm, 4 * n + i + 1)
                    for k in (2 * i, 2 * i + 1):
                        g, b = C_LNG + n * KD + k, C_LNB + n * KD + k
                        last = V.tensor_scalar(hT[:, k, :], bank[t_bank(n) + i][:, (k % 2) * S:(k % 2 + 1) * S],
                                               cst[:, g:g + 1], cst[:, b:b + 1], ALU.mult, ALU.add)
                    if n == 1:
                        link(last)
                        last = V.tensor_copy(aT_high[:, 2 * i:2 * i + 2, :], hT[:, 2 * i:2 * i + 2, :])
                    last.then_inc(hT_v, 1)
                if n == 1:
                    for i in range(4):
                        if i % 2 == 0:
                            dve.wait_ge(hT_a, 2 * n + i // 2 + 1)
                        else:
                            dve.wait_ge(hT_v, 2 * n + i // 2 + 1)
                        two = slice(2 * i, 2 * i + 2)
                        V.tensor_tensor(aT_low[:, two, :], hT[:, two, :], aT_high[:, two, :],
                                        ALU.subtract).then_inc(aT_rest, 1)

            def slots(n):
                return iota.unsqueeze(1).unsqueeze(1).to_broadcast([P, TB, n, CAP])

            def of_pair(table, q):
                return table[:, :, bass.ds(q * 2, 2)].unsqueeze(3).to_broadcast([P, TB, 2, CAP])

            def select(m, r):
                V.tensor_tensor(sel.rearrange("p t (e c) -> p t e c", e=2), slots(2), r,
                                ALU.is_equal).then_inc(m["sel"], 1)

            def select_gated(m, q):
                sg = selg.rearrange("p t (e c) -> p t e c", e=2)
                V.tensor_tensor(sg, slots(2), of_pair(rank_item, q), ALU.is_equal).then_inc(m["end"], 1)
                dve.wait_ge(m["end"], q + 1)
                V.tensor_tensor(sg, sg, of_pair(gate_item, q), ALU.mult)

            def copy_exT(m, n):
                dve.wait_ge(m["gathered"], n)
                V.tensor_copy(exT[:, 4:8, :], bank[1][:, :].rearrange("p (k c) -> p k c", k=4)
                              ).then_inc(m["exT_v"], 1)

            def expert_pair(m, q, following):
                dve.wait_ge(m["silu"], q + 1)
                dve.wait_ge(m["up"], q + 1)
                V.tensor_tensor(hid[:, :], silu_g[:, :], bank[3][:, :], ALU.mult).then_inc(m["hid"], 1)
                if following:
                    copy_exT(m, q + 2)
                dve.wait_ge(m["tr"], q + 1)
                V.tensor_copy(hidT.rearrange("p k c -> p (k c)"), bank[4][:, :]).then_inc(m["hidT"], 1)
                if following:
                    select_gated(m, q + 1)
                    select(m, of_pair(rank_item, q + 2))
                dve.wait_ge(m["down"], q + 1)
                V.tensor_copy(yex[:, 512:1024], bank[6][:, :]).then_inc(m["yex_v"], 1)
                for i, (t, c) in enumerate(((0, 0), (0, 1), (1, 0), (1, 1))):
                    dve.wait_ge(m["comb"], q * 4 + (i + 1))
                    a = yacc[:, t, c * 512:(c + 1) * 512]
                    V.tensor_tensor(a, a, bank[7 if i % 2 == 0 else 4][:, :], ALU.add).then_inc(m["added"], 1)

            def experts(L):
                m = moe[L]
                T = V.tensor_tensor
                r3 = lambda a, n, w: rt[:, a:a + 2 * n].rearrange("p (t e) -> p t e", t=TB)
                mask = r3(0, E, 0)
                ge = r3(64, 4, 0)
                dd = rt[:, 72:74].rearrange("p (t e) -> p t e", t=TB)
                lg = r3(80, 36, 0)
                gpad = r3(152, 8, 0)
                gtop = r3(168, 8, 0)
                goh = r3(184, 4, 0)
                gval = r3(192, 1, 0)
                sl = r3(200, 8, 0)
                etop = r3(216, 8, 0)
                fi = r3(232, 8, 0)
                oh0 = r3(248, 8, 0)
                oh1 = r3(264, 8, 0)
                pr = r3(280, 2, 0)
                rr = r3(284, 1, 0)
                gt = r3(300, E, 0)
                cnt = rt[:, 370:380]
                tmp = rt[:, 400:464].rearrange("p (t g e) -> p t g e", t=TB, g=G)
                link(V.memset(gpad, -3.0e38))
                V.memset(cnt[:, 9:10], 0.0).then_inc(m["hid"], 1)
                dve.wait_ge(m["logit"], 1)
                c = R_RB + L * 36
                link(T(lg, bank[0][:, 0:72].rearrange("p (t e) -> p t e", t=TB),
                       row[:, c:c + 36].unsqueeze(1).to_broadcast([P, TB, 36]), ALU.add))
                link(V.tensor_copy(gpad[:, :, 0:4], lg[:, :, 0:4]))
                ix = idx[:, 0:16].rearrange("p (t e) -> p t e", t=TB)
                for t in range(TB):
                    link(V.max(gtop[:, t, :], gpad[:, t, :]))
                    link(V.max_index(ix[:, t, :], gtop[:, t, :], gpad[:, t, :]))
                T(ge, lg[:, :, 0:4], gtop[:, :, 0:1].to_broadcast([P, TB, 4]), ALU.subtract).then_inc(m["gsub"], 1)
                link(V.tensor_scalar(fi, ix, 1.0, None, ALU.add))
                link(T(goh, iota[:, 0:4].unsqueeze(1).to_broadcast([P, TB, 4]),
                       fi[:, :, 0:1].to_broadcast([P, TB, 4]), ALU.is_equal))
                link(T(tmp, lg[:, :, 4:36].rearrange("p t (g e) -> p t g e", g=G),
                       goh.unsqueeze(3).to_broadcast([P, TB, G, 8]), ALU.mult))
                link(V.tensor_reduce(sl, tmp.rearrange("p t g e -> p t e g"), AX.X, ALU.add))
                for t in range(TB):
                    link(V.max(etop[:, t, :], sl[:, t, :]))
                    link(V.max_index(ix[:, t, :], etop[:, t, :], sl[:, t, :]))
                T(dd, etop[:, :, 1:2], etop[:, :, 0:1], ALU.subtract).then_inc(m["dsub"], 1)
                link(V.tensor_scalar(fi, ix, 1.0, None, ALU.add))
                i8 = iota[:, 0:8].unsqueeze(1).to_broadcast([P, TB, 8])
                link(T(oh0, i8, fi[:, :, 0:1].to_broadcast([P, TB, 8]), ALU.is_equal))
                link(T(oh1, i8, fi[:, :, 1:2].to_broadcast([P, TB, 8]), ALU.is_equal))
                link(T(sl, oh0, oh1, ALU.add))
                T(mask.rearrange("p t (g e) -> p t g e", g=G), goh.unsqueeze(3).to_broadcast([P, TB, G, 8]),
                  sl.unsqueeze(2).to_broadcast([P, TB, G, 8]), ALU.mult).then_inc(m["mask"], 1)
                dve.wait_ge(m["rank"], 1)
                link(T(gt, bank[4][:, 0:2 * E].rearrange("p (t e) -> p t e", t=TB), mask, ALU.mult))
                link(T(gt, gt, mask, ALU.add))
                select(m, gt[:, :, 0:2].unsqueeze(3).to_broadcast([P, TB, 2, CAP]))
                active = rt[:, 380:381]
                T(active, bank[4][:, 2 * E:2 * E + 1], cst[:, C_THR:C_THR + 1], ALU.is_gt).then_inc(m["active"], 1)
                for b in range(NBLK):
                    V.tensor_scalar(tables[:, 0, :, b * E:(b + 1) * E], gt, -1.0 * CAP * b, None, ALU.add)
                dve.wait_ge(m["gexp"], 1)
                link(V.tensor_reduce(gval, ge, AX.X, ALU.add))
                dve.wait_ge(m["dexp"], 1)
                link(V.tensor_scalar(rr, dd, 1.0, None, ALU.add))
                link(T(rr, rr, gval, ALU.mult))
                link(V.reciprocal(pr[:, :, 0:1], rr))
                link(T(pr[:, :, 1:2], pr[:, :, 0:1], dd, ALU.mult))
                link(T(oh0, oh0, pr[:, :, 0:1].to_broadcast([P, TB, 8]), ALU.mult))
                link(T(oh1, oh1, pr[:, :, 1:2].to_broadcast([P, TB, 8]), ALU.mult))
                link(T(oh0, oh0, oh1, ALU.add))
                for b in range(NBLK):
                    ins = T(tables[:, 1, :, b * E:(b + 1) * E].rearrange("p t (g e) -> p t g e", g=G),
                            goh.unsqueeze(3).to_broadcast([P, TB, G, 8]),
                            oh0.unsqueeze(2).to_broadcast([P, TB, G, 8]), ALU.mult)
                ins.then_inc(m["table"], 1)
                dve.wait_ge(m["place"], 1)
                link(T(cnt[:, 0:1], bank[5][:, 0:1], active, ALU.mult))
                link(T(cnt[:, 1:2], cnt[:, 0:1], active, ALU.add))
                T(is_item, iota[:, 0:NITEM], cnt[:, 1:2].to_broadcast([P, NITEM]), ALU.is_equal).then_inc(m["item"], 1)
                copy_exT(m, 1)
                dve.wait_ge(m["listed"], 1)
                link(V.tensor_copy(small[0:1, L, 0:NITEM], bank[5][0:1, 64:64 + NITEM]))
                taken = bank[5][0:1, 130:128 + NITEM].rearrange("p (i two) -> p i two", two=2)
                link(V.tensor_reduce(cnt[0:1, 5:6], taken[:, :, 0], AX.X, ALU.add))
                link(V.tensor_copy(small[0:1, L, NITEM:NITEM + 1], cnt[0:1, 5:6]))
                V.tensor_copy(cnt[:, 6:7], cnt[:, 0:1]).then_inc(m["route"], 1)
                n = TB * NITEM
                link(V.tensor_copy(rank_item.rearrange("p t i -> p (t i)"), bank[7][:, 0:n]))
                link(V.tensor_copy(gate_item.rearrange("p t i -> p (t i)"), bank[7][:, n:2 * n]))
                dve.wait_ge(m["route"], 1)
                further = further_pairs(dve, L)
                select_gated(m, 0)
                select(m, of_pair(rank_item, 1))
                with dve.Fori(0, further) as q:
                    expert_pair(m, q, True)
                expert_pair(m, further, False)
                dve.wait_ge(m["added"], further * 4 + 5)
                return further + 1

            dve.wait_ge(h_in, 16)
            layer_norm(0, h, lambda t, c: bank[4 + 2 * t + c][:, :], lnst)
            copy_hT(0)
            pairs0 = experts(0)
            layer_norm(1, yacc, None, lnst)
            copy_hT(1)
            def projected(u):
                dve.wait_ge(att["proj"], u + 1)
                V.tensor_copy(unit_buffer(u), bank[u % 2][:, 0:512 if UNITS[u][0] == "V" else S]
                              ).then_inc(att["ev_v"], 1)

            def logits(n):
                dve.wait_ge(att["score"], n + 1)
                if n >= 2:
                    dve.wait_ge(att["pt"], n - 1)
                s = scb[:, n % 2, :]
                V.scalar_tensor_tensor(s[:, 0:P], bank[4 + n % 2][:, 0:P], SCALE, bias[:, n, P:S],
                                       ALU.mult, ALU.add)
                link(V.scalar_tensor_tensor(s[:, P:384], bank[4 + n % 2][:, P:384], SCALE, bias[:, n, :],
                                            ALU.mult, ALU.add))
                V.tensor_reduce(am[:, 0, 0, n:n + 1], s[:, 0:P], AX.X, ALU.max)
                link(V.tensor_reduce(am[:, 0, 1, n:n + 1], s[:, P:384], AX.X, ALU.max))
                V.tensor_scalar(am[:, 1, :, n:n + 1], am[:, 0, :, n:n + 1], -1.0, None,
                                ALU.mult).then_inc(att["negmax"], 1)

            dve.wait_ge(att["bias"], 8)
            for kind, n in ATT_ORDER:
                if kind == "project" and n % 2 == 1:
                    projected(n)
                elif kind == "scores":
                    logits(n)
            dve.wait_ge(att["ln"], 1)
            link(V.tensor_tensor(am[:, 4, :, :], am[:, 3, :, :], am[:, 0, :, :], ALU.add))
            for i, (a, n) in enumerate(AGROUPS):
                link(V.tensor_reduce(am[:, 5, :, i:i + 1], am[:, 4, :, a:a + n], AX.X, ALU.add))
                link(V.tensor_scalar(am[:, 5, :, i:i + 1], am[:, 5, :, i:i + 1], 1.0 / n, None, ALU.mult))
            link(V.tensor_reduce(am[:, 7, :, 0:1], am[:, 5, :, 0:3], AX.X, ALU.max))
            V.tensor_tensor(am[:, 6, :, 0:3], am[:, 5, :, 0:3], am[:, 7, :, 0:1].to_broadcast([P, TB, 3]),
                            ALU.subtract).then_inc(att["lse"], 1)
            dve.wait_ge(att["wexp"], 1)
            link(V.tensor_reduce(am[:, 7, :, 1:2], am[:, 6, :, 0:3], AX.X, ALU.add))
            link(V.reciprocal(am[:, 7, :, 2:3], am[:, 7, :, 1:2]))
            link(V.tensor_scalar(am[:, 7, :, 2:3], am[:, 7, :, 2:3], 3.0, None, ALU.mult))
            link(V.tensor_tensor(am[:, 6, :, 0:3], am[:, 6, :, 0:3], am[:, 7, :, 2:3].to_broadcast([P, TB, 3]),
                                 ALU.mult))
            link(V.reciprocal(am[:, 8, :, :], am[:, 2, :, :]))
            for i, (a, n) in enumerate(AGROUPS):
                link(V.tensor_tensor(am[:, 8, :, a:a + n], am[:, 8, :, a:a + n],
                                     am[:, 6, :, i:i + 1].to_broadcast([P, TB, n]), ALU.mult))
            dve.wait_ge(att["oc"], 4)
            for t in range(TB):
                o4 = osb[:, t, :].rearrange("p (r c) -> p r c", r=AH)
                V.tensor_tensor(o4, o4, am[:, 8, t, :].unsqueeze(2).to_broadcast([P, AH, HD]),
                                ALU.mult).then_inc(att["o"], 1)
            for i in range(4):
                b = bank[4 + i][:, :].rearrange("p (k s) -> p k s", k=2)
                two = slice(2 * i, 2 * i + 2)
                if i % 2:
                    dve.wait_ge(att["oT"], i + 1)
                    link(V.tensor_copy(oT_high[:, two, :], b))
                else:
                    dve.wait_ge(att["oTa"], i // 2 + 1)
                V.tensor_tensor(oT_low[:, two, :], b, oT_high[:, two, :], ALU.subtract).then_inc(att["oTl"], 1)
            for c in range(4):
                low_chunk(dve, V, w_low_v, J_ATT + 14, c, pairs0)
            layer_norm(2, h, lambda t, c: bank[2 * t + c][:, :], lnst2)
            copy_hT(2)
            experts(1)
            layer_norm(3, yacc, None, lnst)


UNITS = [("K", i, J_ATT, i == 0, i == 3) for i in range(4)]
UNITS += [("Q", i, J_ATT + 2, i == 0, i == 3) for i in range(4)]
UNITS += [("V", i, J_ATT + 4 + 2 * (i // 2), i % 2 == 0, i % 2 == 1) for i in range(4)]
for _i in range(4, 8):
    UNITS += [("K", _i, J_ATT + 8, _i == 4, _i == 7), ("Q", _i, J_ATT + 10, _i == 4, _i == 7)]
CHUNKS_AFTER = {0: 1, 1: 1, 2: 1, 3: 1, 5: 1, 6: 1, 7: 1, 8: 1, 9: 2, 10: 2, 11: 3, 12: 1, 14: 1, 15: 1, 16: 1, 17: 1}
assert sum(CHUNKS_AFTER.values()) == 5 * 4
UNIT_OF_HEADS = [4 + i if i < 4 else 13 + 2 * (i - 4) for i in range(8)]
UNIT_OF_V = [9, 11]


def attention_order():
    order = [("project", u) for u in range(8)] + [("scores", 0), ("scores", 1)]

    def head(n):
        steps = [("turn", n)] if n < AH else []
        steps += [("scores", n + 2)] if n + 2 < AH else []
        return steps + ([("values", n - 1)] if n else [])

    n = 0
    for u in range(8, 20):
        order.append(("project", u))
        for _ in range(2 if u == 10 else 1):
            order += head(n)
            n += 1
    while n <= AH:
        order += head(n)
        n += 1
    return order


ATT_ORDER = attention_order()


def distances():
    y = np.arange(384)
    dist = 255 - y
    n = np.maximum(dist, 1).astype(np.float64)
    large = 16 + (np.log(n / 16) / np.log(2048 / 16) * 16).astype(np.int32)
    bucket = np.where(dist < 16, np.maximum(dist, 0), np.minimum(large, 31))
    onehot = (np.arange(32)[:, None] == bucket[None]).astype(np.float32)
    dil = np.array([1] * 6 + [4] * 5 + [16] * 5)[:, None]
    ok = (dist[None] >= 0) & (dist[None] % dil == 0) & (dist[None] // dil <= 128)
    return onehot, np.where(ok, 0.0, -1.0e30).astype(np.float32)


def kernel(**inputs):
    import concourse.bacc as bacc
    from concourse.bass_utils import run_bass_kernel_spmd as run

    a = {k: np.asarray(v) for k, v in inputs.items()}
    f = np.float32
    ca = np.ascontiguousarray
    lay = lambda w: w.reshape(KD, P, -1).transpose(1, 0, 2).reshape(P, -1)
    k = np.arange(P)
    router = [np.concatenate([a["moe_group_w"][i], a["moe_expert_w"][i].transpose(1, 0, 2).reshape(D, E)], 1)
              for i in range(2)]
    consts = np.concatenate([
        a["ssm_conv_w"][0].reshape(4, 24, P).transpose(2, 1, 0).reshape(P, 96),
        a["ssm_conv_b"][0].reshape(24, P).T,
        a["ssm_norm_w"][0].reshape(16, P).T,
        np.eye(P, dtype=f), (k[:, None] <= k[None]).astype(f), (k[:, None] < k[None]).astype(f),
        np.ones((P, P), f), np.broadcast_to(np.arange(1, CAP + 1, dtype=f), (P, CAP)),
        lay(router[0]), lay(router[1]), lay(a["ssm_in_w"][0][:, 5120:5152]),
        np.eye(P, dtype=f)[::-1], a["ln_g"].reshape(4 * KD, P).T, a["ln_b"].reshape(4 * KD, P).T,
        (k % E).astype(f)[:, None], np.where(k < 2, -1.0, k // E * CAP + 0.5).astype(f)[:, None]], 1)
    rows = np.concatenate([a["ssm_dt_bias"][0], a["ssm_a_log"][0], a["ssm_d"][0]]
                          + [b for i in range(2) for b in (a["moe_group_b"][i], a["moe_expert_b"][i].reshape(-1))])
    onehot, forbidden = distances()
    bias_pack = np.zeros((32, 784), f)
    bias_pack[:, 0:384] = onehot
    bias_pack[0:AH, 384:768] = forbidden
    bias_pack[:, 768:784] = a["rel_bias"]
    arrays = {
        "x": ca(a["x"]), "xT": ca(a["x"][0].T.reshape(KD, P, S).transpose(1, 0, 2)),
        "consts": ca(consts), "rows": ca(rows), "in_w": ca(a["ssm_in_w"][0]), "out_w": ca(a["ssm_out_w"][0]),
        "kv_w": ca(a["kv_w"]), "q_w": ca(a["attn_q_w"][0]), "o_w": ca(a["attn_o_w"][0]), "bias_pack": bias_pack,
        "gate_w": ca(a["moe_gate_w"].reshape(2, E, D, 512)), "up_w": ca(a["moe_up_w"].reshape(2, E, D, 512)),
        "down_w": ca(a["moe_down_w"].reshape(2, E, 512, D)), "ln_g": ca(a["ln_g"]), "ln_b": ca(a["ln_b"]),
    }
    nc = bacc.Bacc("TRN2", target_bir_lowering=False, num_devices=1)
    args = [nc.dram_tensor("in_" + n, v.shape, F32, kind="ExternalInput").ap() for n, v in arrays.items()]
    args.append(nc.dram_tensor("out_0", (1, S, D), F32, kind="ExternalOutput").ap())
    program(nc, *args)
    r = run(nc, [{"in_" + n: v for n, v in arrays.items()}], core_ids=[0])
    return r.results[0]["out_0"]
```
